# Optimizing a Trainium2 kernel written in Bass

```python
import math
import jax, jax.numpy as jnp
from jax import lax
import numpy as np

D_MODEL = 2048
BATCH = 1
SEQ = 256
DEPTH = 1
DEC_BATCH = 8
DEC_SEQ = 1
PAST_LEN = 2048
PAGE_SIZE = 128

HGRN_HEADS = 8
HGRN_DK = 128
HGRN_DV = 128
HGRN_WIDTH = HGRN_HEADS * HGRN_DK
GLA_HEADS = 4
GLA_DK = 128
GLA_DV = 256
GLA_K_WIDTH = GLA_HEADS * GLA_DK
GLA_V_WIDTH = GLA_HEADS * GLA_DV
GLA_GATE_RANK = 16
GLA_GATE_NORM = 16.0
D_FF = 4 * D_MODEL
PLE_DIM = 256
CHUNK = 64
EPS = 1e-6

IN_WIDTHS = [HGRN_WIDTH, HGRN_WIDTH, HGRN_WIDTH, HGRN_WIDTH,
             GLA_K_WIDTH, GLA_K_WIDTH, GLA_V_WIDTH, GLA_V_WIDTH,
             GLA_GATE_RANK,
             D_MODEL, D_MODEL]
N_IN = sum(IN_WIDTHS)
IN_SPLITS = np.cumsum(IN_WIDTHS)[:-1].tolist()

kernel_name = "hgrn2_gla_gated_hybrid_step"

def _rmsnorm(x, g):
    xf = x.astype(jnp.float32)
    y = xf * lax.rsqrt(jnp.mean(xf * xf, axis=-1, keepdims=True) + EPS)
    return (y * g.astype(jnp.float32)).astype(x.dtype)

def _gated_recurrence(q, k, v, log_a, s0):
    B, L, H, K = q.shape
    V = v.shape[-1]
    c = math.gcd(CHUNK, L)
    n = L // c

    def to_blocks(t):
        return t.astype(jnp.float32).reshape(B, n, c, H, t.shape[-1]).transpose(1, 0, 3, 2, 4)

    qc, kc, vc, gc = to_blocks(q), to_blocks(k), to_blocks(v), to_blocks(log_a)
    causal = jnp.tril(jnp.ones((c, c), dtype=bool))[:, :, None]

    def step(s, inp):
        qi, ki, vi, gi = inp
        b = jnp.cumsum(gi, axis=-2)
        diff = b[..., :, None, :] - b[..., None, :, :]
        decay = jnp.exp(jnp.where(causal, diff, -jnp.inf))
        scores = jnp.einsum('bhtk,bhsk,bhtsk->bhts', qi, ki, decay)
        o = (jnp.einsum('bhts,bhsv->bhtv', scores, vi)
             + jnp.einsum('bhtk,bhkv->bhtv', qi * jnp.exp(b), s))
        b_last = b[..., -1:, :]
        s_new = (jnp.exp(b_last[..., 0, :])[..., None] * s
                 + jnp.einsum('bhsk,bhsv->bhkv', ki * jnp.exp(b_last - b), vi))
        return s_new, o

    s_fin, oc = lax.scan(step, s0.astype(jnp.float32), (qc, kc, vc, gc))
    o = oc.transpose(1, 0, 3, 2, 4).reshape(B, L, H, V)
    return o, s_fin

def _layer(h, p_i, s_h0, s_g0, lb_i, n_pre_mix, n_post_mix, n_pre_ffn, n_post_ffn,
           w_in, hgrn_norm, w_hgrn_up, w_gla_gate, b_gla_gate, gla_norm, w_gla_up,
           w_out, w_ff1, w_ff2, w_ple, w_ple_gate):
    B, L, _ = h.shape
    a = _rmsnorm(h, n_pre_mix)
    z = jnp.einsum('bld,dn->bln', a, w_in)
    (zq, zf, zi, zg, gq, gk, gv, gr, glr, m_h, m_g) = jnp.split(z, IN_SPLITS, axis=-1)

    lb = lb_i.reshape(HGRN_HEADS, HGRN_DK).astype(jnp.float32)
    fl = zf.reshape(B, L, HGRN_HEADS, HGRN_DK).astype(jnp.float32)
    log_f = jnp.logaddexp(jnp.log(lb), jnp.log1p(-lb) + jax.nn.log_sigmoid(fl))
    k_h = (1.0 - lb) * jax.nn.sigmoid(-fl)
    q_h = jax.nn.silu(zq).reshape(B, L, HGRN_HEADS, HGRN_DK)
    i_h = zi.reshape(B, L, HGRN_HEADS, HGRN_DV)
    o_h, s_h = _gated_recurrence(q_h, k_h, i_h, log_f, s_h0)
    o_h = _rmsnorm(o_h, hgrn_norm).astype(h.dtype) * jax.nn.silu(zg).reshape(B, L, HGRN_HEADS, HGRN_DV)
    y_h = jnp.einsum('blc,cd->bld', o_h.reshape(B, L, HGRN_WIDTH), w_hgrn_up)

    log_a = jax.nn.log_sigmoid((jnp.einsum('blr,rk->blk', glr, w_gla_gate) + b_gla_gate)
                               .astype(jnp.float32)) / GLA_GATE_NORM
    q_g = (gq * (GLA_DK ** -0.5)).reshape(B, L, GLA_HEADS, GLA_DK)
    k_g = gk.reshape(B, L, GLA_HEADS, GLA_DK)
    v_g = gv.reshape(B, L, GLA_HEADS, GLA_DV)
    o_g, s_g = _gated_recurrence(q_g, k_g, v_g, log_a.reshape(B, L, GLA_HEADS, GLA_DK), s_g0)
    o_g = _rmsnorm(o_g, gla_norm).astype(h.dtype) * jax.nn.silu(gr).reshape(B, L, GLA_HEADS, GLA_DV)
    y_g = jnp.einsum('blc,cd->bld', o_g.reshape(B, L, GLA_V_WIDTH), w_gla_up)

    merged = jax.nn.sigmoid(m_h) * y_h + jax.nn.sigmoid(m_g) * y_g
    h = h + _rmsnorm(jnp.einsum('bld,de->ble', merged, w_out), n_post_mix)

    c = _rmsnorm(h, n_pre_ffn)
    u = jnp.square(jax.nn.relu(jnp.einsum('bld,df->blf', c, w_ff1)))
    h = h + _rmsnorm(jnp.einsum('blf,fd->bld', u, w_ff2), n_post_ffn)

    pe = jnp.einsum('blp,pd->bld', p_i, w_ple)
    h = h + jax.nn.sigmoid(jnp.einsum('bld,de->ble', h, w_ple_gate)) * pe
    return h, s_h, s_g

def setup_inputs(seed: int = 0) -> dict:
    key = jax.random.key(seed)
    ks = jax.random.split(key, 24)
    f32 = jnp.float32
    nrm = lambda k, shape, scale: jax.random.normal(k, shape, f32) * scale
    gain = lambda k, shape: 1.0 + 0.05 * jax.random.normal(k, shape, f32)
    return {
        "x_prompt": nrm(ks[0], (BATCH, SEQ, D_MODEL), 1.0),
        "x_sample": nrm(ks[1], (DEC_BATCH, DEC_SEQ, D_MODEL), 1.0),
        "p_prompt": nrm(ks[2], (DEPTH, BATCH, SEQ, PLE_DIM), 1.0),
        "p_sample": nrm(ks[3], (DEPTH, DEC_BATCH, DEC_SEQ, PLE_DIM), 1.0),
        "state_hgrn": nrm(ks[4], (DEPTH, DEC_BATCH, HGRN_HEADS, HGRN_DK, HGRN_DV), 0.5),
        "state_gla": nrm(ks[5], (DEPTH, DEC_BATCH, GLA_HEADS, GLA_DK, GLA_DV), 0.5),
        "norm_pre_mix": gain(ks[6], (DEPTH, D_MODEL)),
        "norm_post_mix": gain(ks[7], (DEPTH, D_MODEL)),
        "norm_pre_ffn": gain(ks[8], (DEPTH, D_MODEL)),
        "norm_post_ffn": gain(ks[9], (DEPTH, D_MODEL)),
        "w_in": nrm(ks[10], (DEPTH, D_MODEL, N_IN), D_MODEL ** -0.5),
        "lb_param": nrm(ks[11], (DEPTH, HGRN_WIDTH), 0.1),
        "hgrn_norm": gain(ks[12], (DEPTH, HGRN_DV)),
        "w_hgrn_up": nrm(ks[13], (DEPTH, HGRN_WIDTH, D_MODEL), HGRN_WIDTH ** -0.5),
        "w_gla_gate": nrm(ks[14], (DEPTH, GLA_GATE_RANK, GLA_K_WIDTH), GLA_GATE_RANK ** -0.5),
        "b_gla_gate": nrm(ks[15], (DEPTH, GLA_K_WIDTH), 0.1),
        "gla_norm": gain(ks[16], (DEPTH, GLA_DV)),
        "w_gla_up": nrm(ks[17], (DEPTH, GLA_V_WIDTH, D_MODEL), GLA_V_WIDTH ** -0.5),
        "w_out": nrm(ks[18], (DEPTH, D_MODEL, D_MODEL), D_MODEL ** -0.5),
        "w_ff1": nrm(ks[19], (DEPTH, D_MODEL, D_FF), D_MODEL ** -0.5),
        "w_ff2": nrm(ks[20], (DEPTH, D_FF, D_MODEL), D_FF ** -0.5),
        "w_ple": nrm(ks[21], (DEPTH, PLE_DIM, D_MODEL), PLE_DIM ** -0.5),
        "w_ple_gate": nrm(ks[22], (DEPTH, D_MODEL, D_MODEL), D_MODEL ** -0.5),
    }

def reference(x_prompt, x_sample, p_prompt, p_sample, state_hgrn, state_gla,
              norm_pre_mix, norm_post_mix, norm_pre_ffn, norm_post_ffn, w_in, lb_param,
              hgrn_norm, w_hgrn_up, w_gla_gate, b_gla_gate, gla_norm, w_gla_up, w_out,
              w_ff1, w_ff2, w_ple, w_ple_gate):
    lbs = jnp.cumsum(jax.nn.softmax(lb_param.astype(jnp.float32), axis=0), axis=0)
    lbs = lbs - lbs[0:1]
    Bp = x_prompt.shape[0]
    hp, hs = x_prompt, x_sample
    hgrn_p, gla_p, hgrn_s, gla_s = [], [], [], []
    for i in range(DEPTH):
        w_i = (lbs[i], norm_pre_mix[i], norm_post_mix[i], norm_pre_ffn[i], norm_post_ffn[i],
               w_in[i], hgrn_norm[i], w_hgrn_up[i], w_gla_gate[i], b_gla_gate[i], gla_norm[i],
               w_gla_up[i], w_out[i], w_ff1[i], w_ff2[i], w_ple[i], w_ple_gate[i])
        zh = jnp.zeros((Bp, HGRN_HEADS, HGRN_DK, HGRN_DV), jnp.float32)
        zg = jnp.zeros((Bp, GLA_HEADS, GLA_DK, GLA_DV), jnp.float32)
        hp, sh, sg = _layer(hp, p_prompt[i], zh, zg, *w_i)
        hgrn_p.append(sh.astype(state_hgrn.dtype))
        gla_p.append(sg.astype(state_gla.dtype))
        hs, sh, sg = _layer(hs, p_sample[i], state_hgrn[i], state_gla[i], *w_i)
        hgrn_s.append(sh.astype(state_hgrn.dtype))
        gla_s.append(sg.astype(state_gla.dtype))
    return (hp, hs, jnp.stack(hgrn_p), jnp.stack(gla_p), jnp.stack(hgrn_s), jnp.stack(gla_s))


_drawn_inputs = setup_inputs


def setup_inputs(seed=0):
    import zlib

    import numpy as np

    out = dict(_drawn_inputs(seed))
    spreads = {}
    factors = {}
    for name, (base, spread) in spreads.items():
        noise = np.random.default_rng([zlib.crc32(name.encode()), seed]).standard_normal(out[name].shape)
        drawn = base * np.exp(spread * noise) if base else spread * noise
        out[name] = __import__('jax').numpy.asarray(drawn.astype(out[name].dtype))
    for name, factor in factors.items():
        out[name] = (out[name] * factor).astype(out[name].dtype)
    return out
```

```python
from contextlib import ExitStack

import numpy as np

import concourse.bass as bass
from concourse import mybir

P = 128
D_MODEL = 2048
KT = D_MODEL // P
NP_TOK = 256
NS_TOK = 8
TOK = NP_TOK + NS_TOK
HH, GH = 8, 4
HEADS = HH + GH
GDV = 256
RANK = 16
D_FF = 4 * D_MODEL
PLE = 256
EPS = 1e-6
GATE_NORM = 16.0
LEVELS = 8
HALF = [P >> l for l in range(LEVELS)]
CELLS = (LEVELS - 1) * 64

HT = KT // 2
SLAB = HT * P
RING = 4

T_RANK = 0
T_F = 1
T_Q = T_F + HH
T_GQ = T_Q + HH
T_GK = T_GQ + GH
T_V = T_GK + GH
T_HEADS = T_V + HH + 2 * GH
T_UP = T_HEADS + 4 * HEADS
T_OUT = T_UP + KT
T_FF = T_OUT + KT
FF_BLOCKS = D_FF // D_MODEL
T_PLE = T_FF + 2 * KT * FF_BLOCKS
T_GATE = T_PLE + 2
T_END = T_GATE + KT

F32 = mybir.dt.float32
F32R = mybir.dt.float32r
ALU = mybir.AluOpType
ACT = mybir.ActivationFunctionType


def build(nc, t):
    ctx = ExitStack()

    def sb(name, shape, dt=F32):
        return ctx.enter_context(nc.sbuf_tensor(name, shape, dt))

    def sem(name):
        return ctx.enter_context(nc.semaphore(name))

    raw = sb("raw", [P, RING, SLAB])
    whi = sb("whi", [P, RING, SLAB], F32R)
    wlo = sb("wlo", [P, RING, SLAB], F32R)
    a_hi = sb("a_hi", [P, KT, TOK], F32R)
    a_lo = sb("a_lo", [P, KT, TOK], F32R)
    b_hi = sb("b_hi", [P, KT, TOK], F32R)
    b_lo = sb("b_lo", [P, KT, TOK], F32R)
    p_hi, p_lo = a_hi[:, 0:2, :], a_lo[:, 0:2, :]
    room = sb("room", [P, 2 * KT, TOK])
    zf, zq, zk = room[:, 0:HEADS, :], room[:, HEADS:2 * HEADS, :], room[:, 2 * HEADS:2 * HEADS + GH, :]
    x_in = room[:, HEADS:HEADS + KT, :]
    sgz, sgl = room[:, 2 * HEADS + GH:2 * HEADS + GH + 2, :], room[:, 2 * HEADS + GH + 2:2 * KT, :]
    h_res, t_acc = room[:, 0:KT, :], room[:, KT:2 * KT, :]
    r_bc = sb("r_bc", [P, TOK])
    stage = sb("stage", [P, 2, TOK])
    masks = sb("masks", [P, CELLS])
    ident2 = sb("ident2", [P, 2 * P])
    ones = sb("ones", [P, P])
    gains = sb("gains", [P, 4, KT])
    head_gain = sb("head_gain", [P, 3])
    gate_w = sb("gate_w", [RANK, GH * P])
    gate_b = sb("gate_b", [P, GH])
    mask8 = sb("mask8", [NS_TOK, NS_TOK])
    eps_col = sb("eps_col", [P, 1])
    v_st = sb("v_st", [P, 2, TOK])
    ln_b = sb("ln_b", [P, TOK])
    g_b = sb("g_b", [P, TOK])
    cum = sb("cum", [P, NP_TOK])
    k_b = sb("k_b", [P, TOK])
    q_b = sb("q_b", [P, TOK])
    a_col = sb("a_col", [P, NS_TOK])
    kd = sb("kd", [P, NP_TOK])
    kd_tok = sb("kd_tok", [P, 2, P])
    v_tok = sb("v_tok", [P, 2, GDV])
    ks_tok = sb("ks_tok", [NS_TOK, P])
    vs_tok = sb("vs_tok", [NS_TOK, GDV])
    k_diag = sb("k_diag", [NS_TOK, NS_TOK, P])
    lev = sb("lev", [P, LEVELS, 2, P])
    after_heads = lev[:].rearrange("c l s t -> c (l s t)")
    m_in = after_heads[:, 0:4 * TOK].rearrange("c (a b t) -> c a b t", a=2, b=2)
    merged = after_heads[:, 4 * TOK:6 * TOK].rearrange("c (a t) -> c a t", a=2)
    k_pad = sb("k_pad", [P, LEVELS - 1, NP_TOK])
    probs = sb("probs", [P, 2, CELLS])
    probs_d = sb("probs_d", [P, 3, P])
    S = sb("S", [P, 2, 4, GDV])
    s_out = sb("s_out", [P, GDV])
    sq = sb("sq", [P, 2, TOK])
    rs = sb("rs", [P, TOK])
    o_f = sb("o_f", [P, 2, TOK])

    bank = [ctx.enter_context(nc.psum_tensor(f"bank{i}", [P, 512], F32)) for i in range(8)]
    MM = bank[0:2]
    SC = bank[2:4]
    DG, TP = bank[4], bank[5]
    O = bank[6:8]

    slab_landed = [sem(f"slab_landed{i}") for i in range(RING)]
    hi_ready = sem("hi_ready")
    lo_ready = sem("lo_ready")
    slabs_multiplied = sem("slabs_multiplied")
    tiles_drained = sem("tiles_drained")
    x_landed = [sem(f"x_landed{i}") for i in range(4)]
    const_landed = sem("const_landed")
    consts_set = sem("consts_set")
    h_landed = sem("h_landed")
    a_hi_ready, a_lo_ready = sem("a_hi_ready"), sem("a_lo_ready")
    b_hi_ready, b_lo_ready = sem("b_hi_ready"), sem("b_lo_ready")
    squared, summed = sem("squared"), sem("summed")
    norm_sum_ready, root_ready, r_ready = sem("norm_sum_ready"), sem("root_ready"), sem("r_ready")
    gains_landed = sem("gains_landed")
    gates_ready, gates_stored = sem("gates_ready"), sem("gates_stored")
    silu_done = sem("silu_done")
    stage_stored = [sem("stage_stored0"), sem("stage_stored1")]
    v_landed = sem("v_landed")
    s_landed = [sem("s_landed0"), sem("s_landed1")]
    s_stored = [sem("s_stored0"), sem("s_stored1")]
    state_stored = sem("state_stored")
    by_engine = {
        "act": ["abs_done", "exp_abs_done", "ln_done", "kq_ready", "a_ready", "v_tok_ready", "s_tok_ready",
                "lev_exp", "kd_exp", "kd_tok_ready", "probs0_ready", "sq_ready", "ln_rs", "rs_ready",
                "o_hi_done", "s_out_ready", "sg_abs", "sg_exp", "sg_ln", "sg_sigma"],
        "dve": ["ls_done", "gate_done", "cum_ready", "lev_sub", "lev_ready", "kd_ready",
                "s_new0", "s_new1", "probs_ready", "sg_ls", "sg_ready", "o_scaled",
                "o_gated", "o_done"],
        "pe": ["v_turned", "s_turned", "outer0", "outer1", "so_done", "scores_done", "kd_turned",
               "pv_done", "state_done", "ss_done"],
        "pool": ["k_diag_ready"],
    }
    h_sem = {n: sem(n) for names in by_engine.values() for n in names}
    m_landed = [sem("m_landed0"), sem("m_landed1")]
    sigma_ready, merge_ready = sem("sigma_ready"), sem("merge_ready")
    ht_ready, h_ready = sem("ht_ready"), sem("h_ready")
    u_ready = sem("u_ready")
    p_landed, p_hi_ready, p_lo_ready = sem("p_landed"), sem("p_hi_ready"), sem("p_lo_ready")
    pe_stored = sem("pe_stored")
    gate_pe, y_ready = sem("gate_pe"), sem("y_ready")
    y_stored = [sem("y_stored0"), sem("y_stored1")]

    def outer_at(D, r, i):
        if D == 1:
            return SC[r][:, i * P:(i + 1) * P]
        return SC[i // 2][:, (i % 2) * GDV:(i % 2 + 1) * GDV]

    PE_BANKS = [SC[0], SC[1], DG, O[0]]

    def now(H):
        return H + 2

    def before(H):
        return H + 1

    def tokens(ap, h, side):
        return ap.rearrange("c (p w j) -> c p w j", w=2, j=h)[:, :, side, :]

    def slot_of(par, half):
        return 2 * par + half

    def load(sp, T, par, first=False):
        for half in range(2):
            s = slot_of(par, half)
            if not first:
                sp.wait_ge(lo_ready, 2 * T + (half - RING + 1))
            sp.dma_start(raw[:, s, :], t["stream"][T, :, half * SLAB:(half + 1) * SLAB]).then_inc(slab_landed[s], 16)

    def round_slab(act, T, par, half, first=False):
        s = slot_of(par, half)
        act.wait_ge(slab_landed[s], 8 * T + (16 - 8 * par))
        if not first:
            act.wait_ge(slabs_multiplied, 2 * T + (half - RING + 1))
        act.copy(whi[:, s, :], raw[:, s, :]).then_inc(hi_ready, 1)

    def rest_slab(dve, T, par, half):
        s = slot_of(par, half)
        dve.wait_ge(hi_ready, 2 * T + (half + 1))
        dve.tensor_tensor(wlo[:, s, :], raw[:, s, :], whi[:, s, :].bitcast(F32), ALU.subtract).then_inc(lo_ready, 1)

    def multiply(pe, T, par, half, out, hi, lo, k0, start, stop, before_k=None):
        s = slot_of(par, half)
        pe.wait_ge(lo_ready, 2 * T + (half + 1))
        for k in range(HT):
            if before_k:
                before_k(k0 + k)
            w = slice(k * P, (k + 1) * P)
            pe.matmul(out, whi[:, s, w], hi[:, k0 + k, :], start=start and k == 0, stop=False)
            pe.matmul(out, whi[:, s, w], lo[:, k0 + k, :], start=False, stop=False)
            mm = pe.matmul(out, wlo[:, s, w], hi[:, k0 + k, :], start=False, stop=stop and k == HT - 1)
        mm.then_inc(slabs_multiplied, 1)

    def tile(pe, T, par, hi, lo, first=False, before_half=None, before_k=None):
        if not first:
            pe.wait_ge(tiles_drained, T - 1)
        for half in range(2):
            if before_half:
                before_half(half)
            multiply(pe, T, par, half, MM[par][:, 0:TOK], hi, lo, half * HT, half == 0, half == 1, before_k)

    def tiles(eng, first, last, body):
        with eng.Fori(first, last, 2) as T:
            for j in range(2):
                body(T + j, (first + j) % 2)

    def tile_done(eng, T):
        eng.wait_ge(slabs_multiplied, 2 * T + 2)

    block = ctx.enter_context(nc.Block())

    @block.sync
    def _(sp):
        for i in range(4):
            sp.dma_start(x_in[:, 4 * i:4 * i + 4, :], t["x"][:, 4 * i:4 * i + 4, :]).then_inc(x_landed[i], 16)
            if i == 0:
                sp.dma_start(gains[:], t["gains"]).then_inc(gains_landed, 16)
            if i < 2:
                load(sp, i, i, first=True)
        for dst, name in ((masks, "masks"), (ident2, "ident2"), (head_gain, "head_gain"), (gate_w, "gate_w"),
                          (gate_b, "gate_b"), (mask8, "mask8")):
            sp.dma_start(dst[:], t[name]).then_inc(const_landed, 16)
        load(sp, 2, 0)
        tiles(sp, 3, T_HEADS + 1, lambda T, par: load(sp, T, par))

        def head_loads(H, gla):
            T = 4 * H + T_HEADS
            if gla:
                v = t["v_spill"][:, bass.ds(2 * H - HH, 2), :]
            else:
                v = t["v_spill"][:, bass.ds(H, 1), :]
            sp.wait_ge(h_sem["s_turned"], before(H))
            sp.dma_start(v_st[:, 0:(2 if gla else 1), :], v).then_inc(v_landed, 16)
            load(sp, T + 2, (T_HEADS + 2) % 2)
            sp.wait_ge(h_sem["so_done"], before(H))
            for r in range(2):
                sp.wait_ge(s_stored[r], 16 * H + 16)
                src = t["state_gla"][4 * r:4 * r + 4, H - HH] if gla else t["state_hgrn"][4 * r:4 * r + 4, H]
                w = GDV if gla else P
                sp.dma_start(S[:, r, :, 0:w], src.rearrange("b k v -> k b v")).then_inc(s_landed[r], 16)
            for j in range(3, 6):
                load(sp, T + j, (T_HEADS + j) % 2)

        sp.wait_ge(stage_stored[0], 16 * (1 + HH))
        sp.wait_ge(stage_stored[1], 16 * (1 + HH))
        with sp.Fori(0, HH) as H:
            head_loads(H, False)
        with sp.Fori(HH, HEADS) as H:
            head_loads(H, True)

        sp.wait_ge(stage_stored[0], 16 * (1 + HH + 2 * HH + GH))
        sp.wait_ge(stage_stored[1], 16 * (1 + HH + HH + GH))

        def up_loads(T, par):
            load(sp, T + 2, par)
            sp.wait_ge(merge_ready, T - T_UP + 1)
            sp.dma_start(m_in[:, par_of_m(par), :, :], t["m_spill"][:, bass.ds(2 * (T - T_UP), 2), :])\
              .then_inc(m_landed[par_of_m(par)], 16)

        def par_of_m(par):
            return (par - T_UP) % 2

        tiles(sp, T_UP, T_OUT - 1, up_loads)
        sp.wait_ge(h_sem["o_done"], now(HEADS - 1))
        for i in range(4):
            sp.dma_start(h_res[:, 4 * i:4 * i + 4, :], t["x"][:, 4 * i:4 * i + 4, :]).then_inc(h_landed, 16)
        sp.dma_start(stage[:], t["p"]).then_inc(p_landed, 16)
        tiles(sp, T_OUT + 2, T_END - 1, lambda T, par: load(sp, T, par))

    @block.tensor
    def _(pe):
        for n in by_engine["pe"]:
            pe.sem_inc(h_sem[n], 1)

        tile(pe, T_RANK, 0, a_hi, a_lo, first=True, before_k=lambda k: pe.wait_ge(a_lo_ready, k + 1))
        pe.wait_ge(consts_set, 1)
        pe.wait_ge(summed, KT)
        pe.matmul(TP[:, 0:TOK], ones[:], sq[:, 1, :], start=True, stop=True).then_inc(norm_sum_ready, 1)
        tile(pe, T_F, 1, a_hi, a_lo, first=True)
        pe.wait_ge(tiles_drained, 1)
        pe.wait_ge(const_landed, 16 * 6)
        for h in range(GH):
            mm = pe.matmul(PE_BANKS[h][:, 0:TOK], gate_w[:, h * P:(h + 1) * P], ln_b[0:RANK, :],
                           start=True, stop=True)
        mm.then_inc(gates_ready, 1)
        tile(pe, T_F + 1, 0, a_hi, a_lo)
        tiles(pe, T_F + 2, T_HEADS - 1, lambda T, par: tile(pe, T, par, a_hi, a_lo))

        def turn_v(H, D):
            pe.wait_ge(v_landed, 16 * H + 16)
            pe.wait_ge(h_sem["s_out_ready"], before(H))
            for B in range(2):
                for d in range(D):
                    mm = pe.transpose(TP[:, (B * D + d) * P:(B * D + d + 1) * P], v_st[:, d, B * P:(B + 1) * P],
                                      ident2[:, 0:P])
            mm.then_inc(h_sem["v_turned"], 1)

        def turn_s(H, D):
            pe.wait_ge(h_sem["kq_ready"], now(H))
            pe.wait_ge(h_sem["o_done"], before(H))
            pe.transpose(O[0][0:NS_TOK, 0:P], k_b[:, NP_TOK:TOK], ident2[:, 0:P])
            for d in range(D):
                mm = pe.transpose(O[0][0:NS_TOK, (1 + d) * P:(2 + d) * P], v_st[:, d, NP_TOK:TOK], ident2[:, 0:P])
            mm.then_inc(h_sem["s_turned"], 1)

        def outer(H, D, r):
            if r == 0:
                pe.wait_ge(h_sem["k_diag_ready"], now(H))
                pe.wait_ge(h_sem["probs_ready"], before(H))
            elif D == 2:
                pe.wait_ge(h_sem["s_new0"], now(H))
            for i in range(4):
                mm = pe.matmul(outer_at(D, r, i), k_diag[:, 4 * r + i, :], vs_tok[:, 0:D * P], start=True, stop=True)
            mm.then_inc(h_sem[f"outer{r}"], 1)

        def sample_out(H, D):
            pe.wait_ge(h_sem["s_new1"], now(H))
            for r in range(2):
                for i in range(4):
                    for d in range(D):
                        b = NP_TOK + 4 * r + i
                        mm = pe.matmul(O[d][:, b:b + 1], S[:, r, i, d * P:(d + 1) * P], q_b[:, b:b + 1],
                                       start=(r == 0 and i == 0), stop=True, skip_group_check=True)
            mm.then_inc(h_sem["so_done"], 1)

        def scores(H, D):
            pe.wait_ge(h_sem["lev_ready"], now(H))
            pe.wait_ge(h_sem["s_new1"], now(H))
            pe.wait_ge(h_sem["ln_rs"], before(H))
            for B in range(2):
                at = slice(B * P, (B + 1) * P)
                pe.matmul(DG[:, at], k_b[:, at], q_b[:, at], start=True, stop=True)
                for l in range(1, LEVELS):
                    pe.matmul(SC[B][:, (l - 1) * 64:l * 64], k_pad[:, l - 1, at], lev[:, l, 0, B * 64:(B + 1) * 64],
                              start=True, stop=True)
            pe.matmul(DG[:, 2 * P:3 * P], lev[:, 0, 1, :], lev[:, 0, 0, :], start=True, stop=True)\
              .then_inc(h_sem["scores_done"], 1)

        def turn_kd(H):
            pe.wait_ge(h_sem["kd_ready"], now(H))
            pe.wait_ge(h_sem["v_tok_ready"], now(H))
            for B in range(2):
                mm = pe.transpose(TP[:, B * P:(B + 1) * P], kd[:, B * P:(B + 1) * P], ident2[:, 0:P])
            mm.then_inc(h_sem["kd_turned"], 1)

        def prob_v(H, D):
            pe.wait_ge(h_sem["probs_ready"], now(H))
            pe.wait_ge(h_sem["probs0_ready"], now(H))
            for d in range(D):
                for B in range(2):
                    v = v_tok[:, B, d * P:(d + 1) * P]
                    out = O[d][:, B * P:(B + 1) * P]
                    pe.matmul(out, v, probs_d[:, B, :], start=False, stop=False, skip_group_check=True)
                    for l in range(1, LEVELS):
                        pe.matmul(tokens(out, HALF[l], 1), v,
                                  probs[:, B, (l - 1) * 64:l * 64].rearrange("s (p j) -> s p j", j=HALF[l]),
                                  start=False, stop=False, skip_group_check=True)
                mm = pe.matmul(O[d][:, P:2 * P], v_tok[:, 0, d * P:(d + 1) * P], probs_d[:, 2, :],
                               start=False, stop=True, skip_group_check=True)
            mm.then_inc(h_sem["pv_done"], 1)

        def state(H, D):
            pe.wait_ge(h_sem["kd_tok_ready"], now(H))
            for B in range(2):
                mm = pe.matmul(TP[:, 0:D * P], kd_tok[:, B, :], v_tok[:, B, 0:D * P], start=B == 0, stop=B == 1)
            mm.then_inc(h_sem["state_done"], 1)

        def head_norm(H, D):
            pe.wait_ge(h_sem["sq_ready"], now(H))
            for d in range(D):
                mm = pe.matmul(DG[:, 0:TOK], ones[:], sq[:, d, :], start=d == 0, stop=d == D - 1)
            mm.then_inc(h_sem["ss_done"], 1)

        def head(H, D):
            T = 4 * H + T_HEADS
            after = {0: [lambda: turn_v(H, D)], 1: [lambda: turn_s(H, D)], 2: [lambda: outer(H, D, 0)],
                     3: [lambda: outer(H, D, 1)], 4: [lambda: sample_out(H, D), lambda: turn_kd(H)],
                     5: [lambda: scores(H, D)], 6: [lambda: prob_v(H, D), lambda: state(H, D)],
                     7: [lambda: head_norm(H, D)]}
            for j in range(4):
                par = (T_HEADS + j) % 2
                pe.wait_ge(tiles_drained, T + (j - 1))
                for half in range(2):
                    multiply(pe, T + j, par, half, MM[par][:, 0:TOK], a_hi, a_lo, half * HT, half == 0, half == 1)
                    for f in after[2 * j + half]:
                        f()

        with pe.Fori(0, HH) as H:
            head(H, 1)
        with pe.Fori(HH, HEADS) as H:
            head(H, 2)

        pe.wait_ge(h_sem["o_done"], now(HEADS - 1))

        def up(T, par):
            pe.wait_ge(tiles_drained, T - 1)
            multiply(pe, T, par, 0, MM[par][:, 0:TOK], b_hi, b_lo, 0, True, True)
            multiply(pe, T, par, 1, SC[par][:, 0:TOK], b_hi, b_lo, HT, True, True)

        tiles(pe, T_UP, T_OUT - 1, up)

        def out_proj(T, par):
            tile(pe, T, par, a_hi, a_lo, before_half=lambda half: pe.wait_ge(a_lo_ready, KT + HT * (half + 1)))

        tiles(pe, T_OUT, T_FF - 1, out_proj)

        def norm_sum(n):
            pe.wait_ge(summed, KT * (n + 1))
            pe.matmul(TP[:, 0:TOK], ones[:], sq[:, 1, :], start=True, stop=True).then_inc(norm_sum_ready, 1)

        norm_sum(1)
        for j in range(FF_BLOCKS):
            T0 = T_FF + 2 * KT * j
            if j == 0:
                tile(pe, T0, T0 % 2, b_hi, b_lo, before_k=lambda k: pe.wait_ge(b_lo_ready, k + 1))
                norm_sum(2)
                tile(pe, T0 + 1, (T0 + 1) % 2, b_hi, b_lo)
            tiles(pe, T0 + 2 * (j == 0), T0 + KT - 1, lambda T, par: tile(pe, T, par, b_hi, b_lo))
            tiles(pe, T0 + KT, T0 + 2 * KT - 1, lambda T, par: tile(
                pe, T, par, a_hi, a_lo,
                before_half=lambda half: pe.wait_ge(a_lo_ready, KT * (2 + j) + HT * (half + 1))))

        norm_sum(3)
        pe.wait_ge(p_lo_ready, 1)
        for i in range(4):
            T, half = T_PLE + i // 2, i % 2
            s = slot_of(T % 2, half)
            pe.wait_ge(lo_ready, 2 * T + half + 1)
            for o in range(4):
                if i >= 1:
                    pe.wait_ge(pe_stored, 4 * (i - 1) + o + 1)
                out = PE_BANKS[o][:, 0:TOK]
                for k in range(2):
                    w = slice((2 * o + k) * P, (2 * o + k + 1) * P)
                    pe.matmul(out, whi[:, s, w], p_hi[:, k, :], start=k == 0, stop=False)
                    pe.matmul(out, whi[:, s, w], p_lo[:, k, :], start=False, stop=False)
                    mm = pe.matmul(out, wlo[:, s, w], p_hi[:, k, :], start=False, stop=k == 1)
            mm.then_inc(slabs_multiplied, 1)
        pe.wait_ge(tiles_drained, T_PLE)
        for j in range(2):
            T = T_GATE + j
            tile(pe, T, T % 2, b_hi, b_lo, first=True, before_k=(lambda k: pe.wait_ge(b_lo_ready, KT + k + 1)) if j == 0 else None)
        tiles(pe, T_GATE + 2, T_END - 1, lambda T, par: tile(pe, T, par, b_hi, b_lo))

    @block.scalar
    def _(act):
        for n in by_engine["act"]:
            act.sem_inc(h_sem[n], 1)
        for s in (*stage_stored, *s_stored, state_stored):
            act.sem_inc(s, 16)

        def split(T, par):
            for half in range(2):
                round_slab(act, T, par, half)

        act.wait_ge(gains_landed, 16)
        for k in range(KT):
            if k % 4 == 0:
                act.wait_ge(x_landed[k // 4], 16)
            if k in (4, 8):
                round_slab(act, 0, 0, k // 4 - 1, first=True)
            act.activation(a_hi[:, k, :], x_in[:, k, :], ACT.Identity, scale=gains[:, 0, k:k + 1]).then_inc(a_hi_ready, 1)
        for half in range(2):
            round_slab(act, 1, 1, half, first=True)

        def root(n):
            act.wait_ge(norm_sum_ready, n + 1)
            act.activation(rs[:], TP[:, 0:TOK], ACT.Sqrt, scale=1.0 / D_MODEL, bias=eps_col[:]).then_inc(root_ready, 1)

        act.wait_ge(consts_set, 1)
        root(0)
        split(2, 0)
        act.wait_ge(gates_ready, 1)
        for h in range(GH):
            src = PE_BANKS[h][:, 0:TOK]
            act.activation(zf[:, HH + h, :], src, ACT.Identity, bias=gate_b[:, h:h + 1]).then_inc(gates_stored, 1)
        split(3, 1)
        tiles(act, T_F + 2, T_Q - 1, lambda T, par: split(T + 1, 1 - par))

        def q_tile(T, par):
            split(T + 1, 1 - par)
            act.wait_ge(tiles_drained, T + 1)
            act.activation(zq[:, T - T_Q, :], stage[:, par, :], ACT.Silu).then_inc(silu_done, 1)

        tiles(act, T_Q, T_GQ - 1, q_tile)
        tiles(act, T_GQ, T_V - 1, lambda T, par: split(T + 1, 1 - par))

        def spill(T, par, to, at):
            act.wait_ge(tiles_drained, T + 1)
            act.dma_start(t[to][:, at, :], stage[:, par, :]).then_inc(stage_stored[par], 16)

        def v_tile(T, par):
            split(T + 1, 1 - par)
            spill(T, par, "v_spill", T - T_V)

        tiles(act, T_V, T_HEADS - 1, v_tile)

        act.wait_ge(tiles_drained, T_V)
        act.wait_ge(silu_done, 2 + HH)

        def log_sigmoid(src, buf, names, H):
            act.activation(buf, src, ACT.Abs).then_inc(h_sem[names[0]], 1)
            act.wait_ge(h_sem[names[0]], now(H))
            act.activation(buf, buf, ACT.Exp, scale=-1.0).then_inc(h_sem[names[1]], 1)
            act.wait_ge(h_sem[names[1]], now(H))
            act.activation(buf, buf, ACT.Ln, bias=ones[:, 0:1]).then_inc(h_sem[names[2]], 1)

        def head(H, D):
            T = 4 * H + T_HEADS
            new = t["new_hgrn_sample" if D == 1 else "new_gla_sample"]
            h = H if D == 1 else H - HH

            def store(r):
                act.wait_ge(h_sem[f"s_new{r}"], now(H))
                act.dma_start(new[4 * r:4 * r + 4, h].rearrange("b k v -> k b v"), S[:, r, :, 0:D * P])\
                   .then_inc(s_stored[r], 16)

            def m_spill(j):
                at = 3 * H + (j - 1) if D == 1 else 2 * H + (HH + j - 2)
                spill(T + j, (T_HEADS + j) % 2, "m_spill", at)

            def slab(k):
                round_slab(act, T + (1 + k // 2), (T_HEADS + 1 + k // 2) % 2, k % 2)

            slab(0)
            act.wait_ge(h_sem["ls_done"], before(H))
            log_sigmoid(zf[:, H, :], ln_b[:], ("abs_done", "exp_abs_done", "ln_done"), H)
            act.wait_ge(h_sem["so_done"], before(H))
            act.wait_ge(h_sem["scores_done"], before(H))
            act.copy(q_b[:], zq[:, H, :])
            if D == 1:
                act.wait_ge(h_sem["gate_done"], now(H))
                act.activation(k_b[:], k_b[:], ACT.Exp).then_inc(h_sem["kq_ready"], 1)
            else:
                act.wait_ge(h_sem["kd_ready"], before(H))
                act.copy(k_b[:], zk[:, H - HH, :]).then_inc(h_sem["kq_ready"], 1)
                act.wait_ge(h_sem["gate_done"], now(H))
            act.wait_ge(h_sem["s_new1"], before(H))
            act.activation(a_col[:], g_b[:, NP_TOK:TOK], ACT.Exp).then_inc(h_sem["a_ready"], 1)
            slab(1)
            act.wait_ge(h_sem["v_turned"], now(H))
            act.wait_ge(h_sem["state_done"], before(H))
            act.copy(v_tok[:, :, 0:D * P], TP[:, 0:2 * D * P].rearrange("s (b v) -> s b v", b=2))\
               .then_inc(h_sem["v_tok_ready"], 1)
            act.wait_ge(h_sem["s_turned"], now(H))
            act.wait_ge(h_sem["outer1"], before(H))
            act.copy(ks_tok[:], O[0][0:NS_TOK, 0:P])
            act.copy(vs_tok[:, 0:D * P], O[0][0:NS_TOK, P:(1 + D) * P]).then_inc(h_sem["s_tok_ready"], 1)
            slab(2)
            act.wait_ge(h_sem["cum_ready"], now(H))
            act.wait_ge(h_sem["kd_turned"], before(H))
            act.activation(kd[:], cum[:], ACT.Exp, scale=-1.0, bias=cum[:, NP_TOK - 1:NP_TOK])\
               .then_inc(h_sem["kd_exp"], 1)
            act.wait_ge(h_sem["lev_sub"], now(H))
            act.activation(lev[:], lev[:], ACT.Exp).then_inc(h_sem["lev_exp"], 1)
            slab(3)
            if D == 1:
                act.wait_ge(tiles_drained, T + 1)
                act.wait_ge(h_sem["sg_ready"], before(H))
                log_sigmoid(sgz[:, 0, :], sgl[:, 0, :], ("sg_abs", "sg_exp", "sg_ln"), H)
            slab(4)
            store(0)
            if D == 1:
                m_spill(1)
            else:
                act.wait_ge(tiles_drained, T + 2)
                act.wait_ge(h_sem["sg_ready"], before(H))
                log_sigmoid(sgz[:], sgl[:], ("sg_abs", "sg_exp", "sg_ln"), H)
            act.wait_ge(h_sem["kd_turned"], now(H))
            act.wait_ge(h_sem["state_done"], before(H))
            act.copy(kd_tok[:], TP[:, 0:2 * P].rearrange("s (b k) -> s b k", b=2)).then_inc(h_sem["kd_tok_ready"], 1)
            slab(5)
            store(1)
            act.wait_ge(h_sem["sg_ls"], now(H))
            act.activation(sgl[:, 0:D, :], sgl[:, 0:D, :], ACT.Exp).then_inc(h_sem["sg_sigma"], 1)
            act.wait_ge(h_sem["scores_done"], now(H))
            act.wait_ge(h_sem["pv_done"], before(H))
            act.copy(probs_d[:, 2, :], DG[:, 2 * P:3 * P]).then_inc(h_sem["probs0_ready"], 1)
            slab(6)
            m_spill(2)
            act.wait_ge(h_sem["pv_done"], now(H))
            act.wait_ge(h_sem["ss_done"], before(H))
            for d in range(D):
                sqd = act.activation(sq[:, d, :], O[d][:, 0:TOK], ACT.Square)
            sqd.then_inc(h_sem["sq_ready"], 1)
            act.wait_ge(h_sem["state_done"], now(H))
            act.wait_ge(state_stored, 16 * H + 16)
            act.copy(s_out[:, 0:D * P], TP[:, 0:D * P]).then_inc(h_sem["s_out_ready"], 1)
            act.wait_ge(h_sem["s_out_ready"], now(H))
            act.dma_start(t["new_hgrn_prompt" if D == 1 else "new_gla_prompt"][h], s_out[:, 0:D * P])\
               .then_inc(state_stored, 16)
            slab(7)
            m_spill(3)
            act.wait_ge(h_sem["ss_done"], now(H))
            act.wait_ge(h_sem["o_scaled"], before(H))
            act.activation(rs[:], DG[:, 0:TOK], ACT.Ln, scale=1.0 / (D * P), bias=eps_col[:])\
               .then_inc(h_sem["ln_rs"], 1)
            act.wait_ge(h_sem["ln_rs"], now(H))
            act.activation(rs[:], rs[:], ACT.Exp, scale=-0.5).then_inc(h_sem["rs_ready"], 1)
            act.wait_ge(h_sem["o_gated"], now(H))
            k = H if D == 1 else 2 * H - HH
            act.copy(b_hi[:, bass.ds(k, D), :], o_f[:, 0:D, :]).then_inc(h_sem["o_hi_done"], 1)

        with act.Fori(0, HH) as H:
            head(H, 1)
        with act.Fori(HH, HEADS) as H:
            head(H, 2)

        def merge(T, par):
            split(T + 1, 1 - par)
            m = (par - T_UP) % 2
            act.wait_ge(m_landed[m], 8 * (T - T_UP) + (16 - 8 * m))
            act.activation(m_in[:, m, :, :], m_in[:, m, :, :], ACT.Sigmoid).then_inc(sigma_ready, 1)
            act.wait_ge(merge_ready, T - T_UP + 3)
            act.copy(a_hi[:, T - T_UP, :], merged[:, m, :]).then_inc(a_hi_ready, 1)

        tiles(act, T_UP, T_OUT - 1, merge)
        tiles(act, T_OUT, T_FF - 1, lambda T, par: split(T + 1, 1 - par))

        root(1)
        for k in range(KT):
            act.wait_ge(h_ready, k + 1)
            act.activation(b_hi[:, k, :], h_res[:, k, :], ACT.Identity, scale=gains[:, 2, k:k + 1])\
               .then_inc(b_hi_ready, 1)
        root(2)

        for j in range(FF_BLOCKS):
            T0 = T_FF + 2 * KT * j

            def ff1(T, par):
                split(T + 1, 1 - par)
                i = KT * j + T - T0
                act.wait_ge(tiles_drained, T + 1)
                act.activation(merged[:, par, :], merged[:, par, :], ACT.Square).then_inc(u_ready, 1)
                act.wait_ge(u_ready, i + 1)
                act.copy(a_hi[:, T - T0, :], merged[:, par, :]).then_inc(a_hi_ready, 1)

            tiles(act, T0, T0 + KT - 1, ff1)
            tiles(act, T0 + KT, T0 + 2 * KT - 1, lambda T, par: split(T + 1, 1 - par))

        split(T_PLE + 1, (T_PLE + 1) % 2)
        act.wait_ge(p_landed, 16)
        act.wait_ge(slabs_multiplied, 2 * T_PLE)
        act.copy(p_hi, stage[:]).then_inc(p_hi_ready, 1)
        root(3)
        for k in range(KT):
            act.wait_ge(h_ready, KT + k + 1)
            act.copy(b_hi[:, k, :], h_res[:, k, :]).then_inc(b_hi_ready, 1)
            act.wait_ge(slabs_multiplied, 2 * T_PLE + k // 4 + 1)
            act.copy(t_acc[:, k, :], PE_BANKS[k % 4][:, 0:TOK]).then_inc(pe_stored, 1)
            if k == 7:
                split(T_GATE, T_GATE % 2)
        act.sem_inc(tiles_drained, 2)

        def gate(T, par, last=False):
            if not last:
                split(T + 1, 1 - par)
            tile_done(act, T)
            act.wait_ge(y_ready, T - T_GATE + 1)
            act.activation(sq[:, par, :], MM[par][:, 0:TOK], ACT.Sigmoid).then_inc(tiles_drained, 1)
            n, j = T - T_GATE, (par - T_GATE) % 2
            act.wait_ge(y_ready, n + 3)
            act.dma_start(t["y"][:, n, :], merged[:, j, :]).then_inc(y_stored[j], 16)

        tiles(act, T_GATE, T_END - 3, gate)
        gate(T_END - 2, (T_END - 2) % 2)
        gate(T_END - 1, (T_END - 1) % 2, last=True)
        for j in range(2):
            act.wait_ge(y_stored[j], 16 + 16 * KT // 2)
        for r in range(2):
            act.wait_ge(s_stored[r], 16 * (HEADS + 1))
        act.wait_ge(state_stored, 16 * (HEADS + 1))

    @block.vector
    def _(dve):
        for n in by_engine["dve"]:
            dve.sem_inc(h_sem[n], 1)
        dve.sem_inc(merge_ready, 2)
        dve.sem_inc(y_ready, 2)
        dve.sem_inc(silu_done, 2)

        def split(T, par):
            for half in range(2):
                rest_slab(dve, T, par, half)

        def gained_rest(k, hi, lo, src, gain, ready, done, base=0):
            dve.wait_ge(ready, base + k + 1)
            dve.scalar_tensor_tensor(out=lo[:, k, :], in0=src[:, k, :], scalar=gain, in1=hi[:, k, :].bitcast(F32),
                                     op0=ALU.mult, op1=ALU.subtract).then_inc(done, 1)

        for k in range(KT):
            if k in (4, 8):
                rest_slab(dve, 0, 0, k // 4 - 1)
            gained_rest(k, a_hi, a_lo, x_in, gains[:, 0, k:k + 1], a_hi_ready, a_lo_ready)
        split(1, 1)

        def invert(n):
            dve.wait_ge(root_ready, n + 1)
            dve.reciprocal(r_bc[:], rs[:]).then_inc(r_ready, 1)
            dve.wait_ge(r_ready, n + 1)

        def drain(T, par, out, scale=None, rows=P):
            tile_done(dve, T)
            src = MM[par][0:rows, 0:TOK]
            if scale is None:
                return dve.tensor_tensor(out, src, r_bc[0:rows, :], ALU.mult)
            return dve.scalar_tensor_tensor(out=out, in0=src, scalar=scale, in1=r_bc[:], op0=ALU.mult, op1=ALU.mult)

        invert(0)
        drain(0, 0, ln_b[0:RANK, :], rows=RANK).then_inc(tiles_drained, 1)
        split(2, 0)
        drain(T_F, 1, zf[:, 0, :]).then_inc(tiles_drained, 1)
        split(3, 1)
        drain(T_F + 1, 0, zf[:, 1, :]).then_inc(tiles_drained, 1)

        def stored(base, dst, scale=None):
            def body(T, par):
                split(T + 1, 1 - par)
                drain(T, par, dst[:, T - base, :], scale).then_inc(tiles_drained, 1)
            return body

        tiles(dve, T_F + 2, T_Q - 1, stored(T_F, zf))

        def q_tile(T, par):
            split(T + 1, 1 - par)
            dve.wait_ge(silu_done, T - T_Q + 1)
            drain(T, par, stage[:, par, :]).then_inc(tiles_drained, 1)

        tiles(dve, T_Q, T_GQ - 1, q_tile)
        tiles(dve, T_GQ, T_GK - 1, stored(T_GQ - HH, zq, P ** -0.5))
        tiles(dve, T_GK, T_V - 1, stored(T_GK, zk))
        dve.wait_ge(silu_done, 2 + HH)

        def to_stage(T, par, uses):
            dve.wait_ge(stage_stored[par], 16 * uses + 16)
            drain(T, par, stage[:, par, :]).then_inc(tiles_drained, 1)

        with dve.Fori(0, HH) as i:
            for j in range(2):
                T = 2 * i + (T_V + j)
                par = (T_V + j) % 2
                split(T + 1, 1 - par)
                to_stage(T, par, i)

        dve.wait_ge(gates_stored, GH)
        dve.wait_ge(const_landed, 16 * 6)

        def head(H, D):
            T = 4 * H + T_HEADS

            def slab(k):
                rest_slab(dve, T + (1 + k // 2), (T_HEADS + 1 + k // 2) % 2, k % 2)

            def m_tile(j):
                par = (T_HEADS + j) % 2
                if D == 1:
                    uses = H + HH if par else 2 * H + (HH + (j == 3))
                else:
                    uses = H + HH if par else H + 2 * HH
                to_stage(T + j, par, uses)

            def gate_tile(d):
                last = drain(T + d, (T_HEADS + d) % 2, sgz[:, d, :])
                last.then_inc(tiles_drained, 1)

            slab(0)
            dve.wait_ge(h_sem["ln_done"], now(H))
            dve.wait_ge(h_sem["a_ready"], before(H))
            f = zf[:, H, :]
            dve.scalar_tensor_tensor(out=g_b[:], in0=f, scalar=0.0, in1=ln_b[:], op0=ALU.min, op1=ALU.subtract)\
               .then_inc(h_sem["ls_done"], 1)
            dve.wait_ge(h_sem["ls_done"], now(H))
            dve.wait_ge(h_sem["scores_done"], before(H))
            if D == 1:
                dve.tensor_tensor(k_b[:], g_b[:], f, ALU.subtract).then_inc(h_sem["gate_done"], 1)
            else:
                dve.tensor_scalar(g_b[:], g_b[:], 1.0 / GATE_NORM, None, ALU.mult).then_inc(h_sem["gate_done"], 1)
                dve.wait_ge(h_sem["gate_done"], now(H))
            dve.wait_ge(h_sem["kd_exp"], before(H))
            dve.tensor_tensor_scan(cum[:], ones[:, 0:1].to_broadcast([P, NP_TOK]), g_b[:, 0:NP_TOK], 0.0, ALU.mult, ALU.add)\
               .then_inc(h_sem["cum_ready"], 1)
            slab(1)
            dve.wait_ge(h_sem["cum_ready"], now(H))
            for l in range(LEVELS):
                h = HALF[l]
                pairs = P // h
                left, right = tokens(cum[:], h, 0), tokens(cum[:], h, 1)
                mid = left[:, :, h - 1:h].to_broadcast([P, pairs, h])
                dve.tensor_tensor(lev[:, l, 0, :].rearrange("c (p j) -> c p j", j=h), right, mid, ALU.subtract)
                last = dve.tensor_tensor(lev[:, l, 1, :].rearrange("c (p j) -> c p j", j=h), mid, left, ALU.subtract)
                if l == LEVELS // 2 - 1:
                    slab(2)
            last.then_inc(h_sem["lev_sub"], 1)
            gate_tile(0)
            slab(3)
            dve.wait_ge(h_sem["a_ready"], now(H))

            def new_states(r):
                dve.wait_ge(s_landed[r], 16 * H + 16)
                dve.wait_ge(h_sem[f"outer{r}"], now(H))
                for i in range(4):
                    s = S[:, r, i, 0:D * P]
                    last = dve.scalar_tensor_tensor(out=s, in0=s, scalar=a_col[:, 4 * r + i:4 * r + i + 1],
                                                    in1=outer_at(D, r, i), op0=ALU.mult, op1=ALU.add)
                last.then_inc(h_sem[f"s_new{r}"], 1)

            dve.wait_ge(h_sem["lev_exp"], now(H))
            dve.wait_ge(h_sem["kq_ready"], now(H))
            for l in range(LEVELS):
                h = HALF[l]
                q, k = tokens(q_b[:, 0:NP_TOK], h, 1), tokens(k_b[:, 0:NP_TOK], h, 0)
                lq = lev[:, l, 0, :].rearrange("c (p j) -> c p j", j=h)
                lk = lev[:, l, 1, :].rearrange("c (p j) -> c p j", j=h)
                dve.tensor_tensor(lq, lq, q, ALU.mult)
                k_out = lk if l == 0 else tokens(k_pad[:, l - 1, :], h, 0)
                last = dve.tensor_tensor(k_out, lk, k, ALU.mult)
                if l == 3:
                    new_states(0)
            last.then_inc(h_sem["lev_ready"], 1)
            slab(4)
            if D == 1:
                m_tile(1)
            else:
                gate_tile(1)
            new_states(1)
            dve.wait_ge(h_sem["kd_exp"], now(H))
            dve.tensor_tensor(kd[:], kd[:], k_b[:, 0:NP_TOK], ALU.mult).then_inc(h_sem["kd_ready"], 1)
            slab(5)
            dve.wait_ge(h_sem["sg_ln"], now(H))
            dve.scalar_tensor_tensor(out=sgl[:, 0:D, :], in0=sgz[:, 0:D, :], scalar=0.0, in1=sgl[:, 0:D, :],
                                     op0=ALU.min, op1=ALU.subtract).then_inc(h_sem["sg_ls"], 1)
            slab(6)
            m_tile(2)
            dve.wait_ge(h_sem["scores_done"], now(H))
            dve.wait_ge(h_sem["pv_done"], before(H))
            for B in range(2):
                dve.tensor_tensor(probs[:, B, :], SC[B][:, 0:CELLS], masks[:], ALU.mult)
            dve.tensor_tensor(probs_d[:, 0:2, :], DG[:, 0:2 * P].rearrange("s (b t) -> s b t", b=2),
                              ident2[:].rearrange("s (b t) -> s b t", b=2), ALU.mult).then_inc(h_sem["probs_ready"], 1)
            dve.wait_ge(h_sem["sg_sigma"], now(H))
            dve.tensor_tensor(sgz[:, 0:D, :], sgz[:, 0:D, :], sgl[:, 0:D, :], ALU.mult).then_inc(h_sem["sg_ready"], 1)
            slab(7)
            m_tile(3)
            dve.wait_ge(h_sem["rs_ready"], now(H))
            dve.wait_ge(h_sem["o_hi_done"], before(H))
            for d in range(D):
                gain = head_gain[:, (0 if D == 1 else 1 + d):(1 if D == 1 else 2 + d)]
                last = dve.scalar_tensor_tensor(out=o_f[:, d, :], in0=O[d][:, 0:TOK], scalar=gain, in1=rs[:],
                                                op0=ALU.mult, op1=ALU.mult)
            last.then_inc(h_sem["o_scaled"], 1)
            dve.wait_ge(h_sem["o_scaled"], now(H))
            dve.wait_ge(h_sem["sg_ready"], now(H))
            dve.tensor_tensor(o_f[:, 0:D, :], o_f[:, 0:D, :], sgz[:, 0:D, :], ALU.mult).then_inc(h_sem["o_gated"], 1)
            dve.wait_ge(h_sem["o_hi_done"], now(H))
            k = H if D == 1 else 2 * H - HH
            dve.tensor_tensor(b_lo[:, bass.ds(k, D), :], o_f[:, 0:D, :], b_hi[:, bass.ds(k, D), :].bitcast(F32),
                              ALU.subtract).then_inc(h_sem["o_done"], 1)

        with dve.Fori(0, HH) as H:
            head(H, 1)
        with dve.Fori(HH, HEADS) as H:
            head(H, 2)

        def merge(T, par):
            split(T + 1, 1 - par)
            n, m = T - T_UP, (par - T_UP) % 2
            tile_done(dve, T)
            dve.wait_ge(sigma_ready, n + 1)
            dve.tensor_tensor(m_in[:, m, 0, :], m_in[:, m, 0, :], MM[par][:, 0:TOK], ALU.mult)
            dve.tensor_tensor(m_in[:, m, 1, :], m_in[:, m, 1, :], SC[par][:, 0:TOK], ALU.mult).then_inc(tiles_drained, 1)
            dve.wait_ge(tiles_drained, T + 1)
            dve.tensor_tensor(merged[:, m, :], m_in[:, m, 0, :], m_in[:, m, 1, :], ALU.add).then_inc(merge_ready, 1)
            dve.wait_ge(a_hi_ready, n + (KT + 1))
            dve.tensor_tensor(a_lo[:, n, :], merged[:, m, :], a_hi[:, n, :].bitcast(F32), ALU.subtract)\
               .then_inc(a_lo_ready, 1)

        tiles(dve, T_UP, T_OUT - 1, merge)

        def keep_t(T0, add):
            def body(T, par):
                split(T + 1, 1 - par)
                tile_done(dve, T)
                out = t_acc[:, T - T0, :]
                if add:
                    ins = dve.tensor_tensor(out, out, MM[par][:, 0:TOK], ALU.add)
                else:
                    ins = dve.tensor_copy(out, MM[par][:, 0:TOK])
                ins.then_inc(tiles_drained, 1)
            return body

        tiles(dve, T_OUT, T_FF - 1, keep_t(T_OUT, False))

        def residual(norm, gain_at, gain_next, count):
            for k in range(KT):
                dve.scalar_tensor_tensor(out=t_acc[:, k, :], in0=t_acc[:, k, :], scalar=gains[:, gain_at, k:k + 1],
                                         in1=r_bc[:], op0=ALU.mult, op1=ALU.mult).then_inc(ht_ready, 1)
                if k >= 1:
                    part(k - 1, gain_next, count)
                if k == 9 and count == 1:
                    split(T_GATE, T_GATE % 2)
                dve.wait_ge(ht_ready, KT * count + k + 1)
                dve.tensor_tensor(h_res[:, k, :], h_res[:, k, :], t_acc[:, k, :], ALU.add).then_inc(h_ready, 1)
            part(KT - 1, gain_next, count)

        def part(k, gain, count):
            g = 1.0 if gain is None else gains[:, gain, k:k + 1]
            gained_rest(k, b_hi, b_lo, h_res, g, b_hi_ready, b_lo_ready, KT * count)

        invert(1)
        dve.wait_ge(h_landed, 64)
        residual(1, 1, 2, 0)
        invert(2)

        for j in range(FF_BLOCKS):
            T0 = T_FF + 2 * KT * j

            def ff1(T, par):
                split(T + 1, 1 - par)
                tile_done(dve, T)
                i = KT * j + T - T0
                dve.scalar_tensor_tensor(out=merged[:, par, :], in0=MM[par][:, 0:TOK], scalar=0.0, in1=r_bc[:],
                                         op0=ALU.max, op1=ALU.mult).then_inc(tiles_drained, 1)
                dve.wait_ge(a_hi_ready, i + (2 * KT + 1))
                dve.tensor_tensor(a_lo[:, T - T0, :], merged[:, par, :], a_hi[:, T - T0, :].bitcast(F32),
                                  ALU.subtract).then_inc(a_lo_ready, 1)

            tiles(dve, T0, T0 + KT - 1, ff1)
            tiles(dve, T0 + KT, T0 + 2 * KT - 1, keep_t(T0 + KT, j > 0))

        split(T_PLE + 1, (T_PLE + 1) % 2)
        dve.wait_ge(p_hi_ready, 1)
        dve.tensor_tensor(p_lo, stage[:], p_hi.bitcast(F32), ALU.subtract).then_inc(p_lo_ready, 1)
        invert(3)
        residual(3, 3, None, 1)

        def gate(T, par, last=False):
            if not last:
                split(T + 1, 1 - par)
            n, j = T - T_GATE, (par - T_GATE) % 2
            dve.wait_ge(tiles_drained, T + 1)
            dve.tensor_tensor(sq[:, par, :], sq[:, par, :], t_acc[:, n, :], ALU.mult).then_inc(gate_pe, 1)
            dve.wait_ge(gate_pe, n + 1)
            dve.wait_ge(y_stored[j], 8 * n + (16 - 8 * j))
            dve.tensor_tensor(merged[:, j, :], sq[:, par, :], h_res[:, n, :], ALU.add).then_inc(y_ready, 1)

        dve.sem_inc(y_stored[0], 16)
        dve.sem_inc(y_stored[1], 16)
        tiles(dve, T_GATE, T_END - 3, gate)
        gate(T_END - 2, (T_END - 2) % 2)
        gate(T_END - 1, (T_END - 1) % 2, last=True)

    @block.gpsimd
    def _(pool):
        for n in by_engine["pool"]:
            pool.sem_inc(h_sem[n], 1)
        pool.memset(ones[:], 1.0)
        pool.memset(eps_col[:], EPS).then_inc(consts_set, 1)
        pool.memset(k_pad[:], 0.0).then_inc(consts_set, 1)

        def square(n, k, src):
            first = isinstance(k, int) and k == 0
            out = sq[:, 1, :] if first else sq[:, 0, :]
            done = pool.tensor_tensor(out, src, src, ALU.mult)
            if first:
                done.then_inc(summed, 1)
                return
            done.then_inc(squared, 1)
            pool.wait_ge(squared, k + (KT - 1) * n)
            pool.wait_ge(summed, k + KT * n)
            pool.tensor_tensor(sq[:, 1, :], sq[:, 1, :], sq[:, 0, :], ALU.add).then_inc(summed, 1)
            pool.wait_ge(summed, k + KT * n + 1)

        def squares(n, wait, src):
            for k in range(KT):
                wait(k)
                if k == 0 and n:
                    pool.wait_ge(norm_sum_ready, n)
                square(n, k, src[:, k, :])

        squares(0, lambda k: pool.wait_ge(x_landed[k // 4], 16), x_in)

        pool.wait_ge(const_landed, 16 * 6)

        def head(H, D):

            pool.wait_ge(h_sem["s_tok_ready"], now(H))
            pool.wait_ge(h_sem["outer1"], before(H))
            for b in range(NS_TOK):
                last = pool.tensor_tensor(k_diag[:, b, :], ks_tok[:], mask8[:, b:b + 1].to_broadcast([NS_TOK, P]), ALU.mult)
            last.then_inc(h_sem["k_diag_ready"], 1)

        with pool.Fori(0, HH) as H:
            head(H, 1)
        with pool.Fori(HH, HEADS) as H:
            head(H, 2)

        squares(1, lambda k: pool.wait_ge(tiles_drained, T_OUT + k + 1), t_acc)
        squares(2, lambda k: pool.wait_ge(h_ready, k + 1), h_res)
        squares(3, lambda k: pool.wait_ge(tiles_drained, T_PLE - KT + k + 1), t_acc)

    ctx.close()


def level_masks():
    s, c = np.arange(P)[:, None], np.arange(64)[None, :]
    return np.concatenate([(s // (2 * h) == c // h) for h in HALF[1:]], axis=1).astype(np.float32)


def kernel(**inputs):
    import concourse.bacc as bacc
    from concourse.bass_utils import run_bass_kernel_spmd

    x = {n: np.ascontiguousarray(a) for n, a in inputs.items()}
    f32 = np.float32

    def by_tile(w):
        k, n = w.shape
        return w.reshape(KT, P, n // P, P).transpose(2, 1, 0, 3).reshape(n // P, P, KT * P)

    w_in = x["w_in"][0]
    edges = np.cumsum([0, HH * P, HH * P, HH * P, HH * P, GH * P, GH * P, GH * GDV, GH * GDV, RANK, D_MODEL, D_MODEL])
    zq, zf, zi, zg, gq, gk, gv, gr, glr, m_h, m_g = [w_in[:, a:b] for a, b in zip(edges[:-1], edges[1:])]
    stream = np.empty((T_END, P, KT * P), f32)
    rank = np.zeros((D_MODEL, P), f32)
    rank[:, 0:RANK] = glr
    stream[T_RANK] = by_tile(rank)[0]
    for at, w in ((T_F, zf), (T_Q, zq), (T_GQ, gq), (T_GK, gk), (T_V, zi), (T_V + HH, gv)):
        stream[at:at + w.shape[1] // P] = by_tile(w)
    m = np.stack([by_tile(m_h), by_tile(m_g)], axis=1).reshape(2 * KT, P, KT * P)
    g, r = by_tile(zg), by_tile(gr)
    for h in range(HH):
        stream[T_HEADS + 4 * h] = g[h]
        stream[T_HEADS + 4 * h + 1:T_HEADS + 4 * h + 4] = m[3 * h:3 * h + 3]
    for h in range(GH):
        at = T_HEADS + 4 * (HH + h)
        stream[at:at + 2] = r[2 * h:2 * h + 2]
        stream[at + 2:at + 4] = m[3 * HH + 2 * h:3 * HH + 2 * h + 2]
    up = np.concatenate([x["w_hgrn_up"][0], x["w_gla_up"][0]], axis=0)
    stream[T_UP:T_OUT] = by_tile(up)
    stream[T_OUT:T_FF] = by_tile(x["w_out"][0])
    for j in range(FF_BLOCKS):
        at, b = T_FF + 2 * KT * j, slice(j * D_MODEL, (j + 1) * D_MODEL)
        stream[at:at + KT] = by_tile(x["w_ff1"][0][:, b])
        stream[at + KT:at + 2 * KT] = by_tile(x["w_ff2"][0][b, :])
    ple = x["w_ple"][0].reshape(2, P, 2, KT // 2, P).transpose(2, 1, 3, 0, 4)
    stream[T_PLE:T_GATE] = ple.reshape(2, P, KT * P)
    stream[T_GATE:T_END] = by_tile(x["w_ple_gate"][0])

    def feature_major(prompt, sample):
        a = np.concatenate([prompt.reshape(NP_TOK, -1), sample.reshape(NS_TOK, -1)], axis=0)
        return np.ascontiguousarray(a.T.reshape(-1, P, TOK).transpose(1, 0, 2))

    norms = [x[n][0].reshape(KT, P).T for n in ("norm_pre_mix", "norm_post_mix", "norm_pre_ffn", "norm_post_ffn")]
    arrays = {
        "x": feature_major(x["x_prompt"], x["x_sample"]),
        "p": feature_major(x["p_prompt"], x["p_sample"]),
        "stream": stream,
        "gains": np.ascontiguousarray(np.stack(norms, axis=1)),
        "head_gain": np.ascontiguousarray(np.concatenate([x["hgrn_norm"].T, x["gla_norm"][0].reshape(2, P).T], axis=1)),
        "gate_w": x["w_gla_gate"][0],
        "gate_b": np.ascontiguousarray(x["b_gla_gate"][0].reshape(GH, P).T),
        "state_hgrn": x["state_hgrn"][0],
        "state_gla": x["state_gla"][0],
        "masks": level_masks(),
        "ident2": np.tile(np.eye(P, dtype=f32), (1, 2)),
        "mask8": np.eye(NS_TOK, dtype=f32),
    }
    outs = {
        "y": (P, KT, TOK),
        "new_hgrn_prompt": (HH, P, P),
        "new_gla_prompt": (GH, P, GDV),
        "new_hgrn_sample": (NS_TOK, HH, P, P),
        "new_gla_sample": (NS_TOK, GH, P, GDV),
    }
    nc = bacc.Bacc("TRN2", target_bir_lowering=False, num_devices=1)
    t, sent = {}, {}
    for name, a in arrays.items():
        sent[f"in_{name}"] = a
        t[name] = nc.dram_tensor(f"in_{name}", a.shape, F32, kind="ExternalInput").ap()
    for name, shape in outs.items():
        t[name] = nc.dram_tensor(f"out_{name}", shape, F32, kind="ExternalOutput").ap()
    t["v_spill"] = nc.dram_tensor("v_spill", (P, HH + 2 * GH, TOK), F32, kind="Internal").ap()
    t["m_spill"] = nc.dram_tensor("m_spill", (P, 2 * KT, TOK), F32, kind="Internal").ap()
    build(nc, t)
    got = run_bass_kernel_spmd(nc, [sent], core_ids=[0]).results[0]
    y = got["out_y"].transpose(1, 0, 2).reshape(D_MODEL, TOK).T
    return (np.ascontiguousarray(y[0:NP_TOK]).reshape(x["x_prompt"].shape),
            np.ascontiguousarray(y[NP_TOK:]).reshape(x["x_sample"].shape),
            got["out_new_hgrn_prompt"][None, None], got["out_new_gla_prompt"][None, None],
            got["out_new_hgrn_sample"][None], got["out_new_gla_sample"][None])
```

```python
from contextlib import ExitStack

import numpy as np

import concourse.bass as bass
from concourse import mybir

P = 128
D_MODEL = 2048
KT = D_MODEL // P
NP_TOK = 256
NS_TOK = 8
TOK = NP_TOK + NS_TOK
HH, GH = 8, 4
HEADS = HH + GH
GDV = 256
RANK = 16
D_FF = 4 * D_MODEL
PLE = 256
EPS = 1e-6
GATE_NORM = 16.0
LEVELS = 8
HALF = [P >> l for l in range(LEVELS)]
CELLS = (LEVELS - 1) * 64

HT = KT // 2
SLAB = HT * P
RING = 4

T_RANK = 0
T_F = 1
T_Q = T_F + HH
T_GQ = T_Q + HH
T_GK = T_GQ + GH
T_V = T_GK + GH
T_HEADS = T_V + HH + 2 * GH
T_UP = T_HEADS + 4 * HEADS
T_OUT = T_UP + KT
T_FF = T_OUT + KT
FF_BLOCKS = D_FF // D_MODEL
T_PLE = T_FF + 2 * KT * FF_BLOCKS
T_GATE = T_PLE + 2
T_END = T_GATE + KT

F32 = mybir.dt.float32
F32R = mybir.dt.float32r
ALU = mybir.AluOpType
ACT = mybir.ActivationFunctionType


def build(nc, t):
    ctx = ExitStack()

    def sb(name, shape, dt=F32):
        return ctx.enter_context(nc.sbuf_tensor(name, shape, dt))

    def sem(name):
        return ctx.enter_context(nc.semaphore(name))

    raw = sb("raw", [P, RING, SLAB])
    whi = sb("whi", [P, RING, SLAB], F32R)
    wlo = sb("wlo", [P, RING, SLAB], F32R)
    a_hi = sb("a_hi", [P, KT, TOK], F32R)
    a_lo = sb("a_lo", [P, KT, TOK], F32R)
    with nc.sbuf_tensor("before_b", [P, 2 * KT, TOK], F32) as before_b:
        log_gate = before_b[:, 0:HEADS, :]
        hk = before_b[:, KT + HH:2 * KT, :]
    b_hi = sb("b_hi", [P, KT, TOK], F32R)
    b_lo = sb("b_lo", [P, KT, TOK], F32R)
    p_hi, p_lo = a_hi[:, 0:2, :], a_lo[:, 0:2, :]
    room = sb("room", [P, 2 * KT, TOK])
    zf, zq, zk = room[:, 0:HEADS, :], room[:, HEADS:2 * HEADS, :], room[:, 2 * HEADS:2 * HEADS + GH, :]
    gates = zf
    x_in = room[:, HEADS:HEADS + KT, :]
    sgz, sgl = room[:, 2 * HEADS + GH:2 * HEADS + GH + 2, :], room[:, 2 * HEADS + GH + 2:2 * KT, :]
    h_res, t_acc = room[:, 0:KT, :], room[:, KT:2 * KT, :]
    r_bc = sb("r_bc", [P, TOK])
    stage = sb("stage", [P, 2, TOK])
    masks = sb("masks", [P, CELLS])
    ident = sb("ident", [P, 3 * P])
    ones = sb("ones", [P, P])
    gains = sb("gains", [P, 4, KT])
    head_gain = sb("head_gain", [P, 3])
    gate_w = sb("gate_w", [RANK, GH * P])
    gate_b = sb("gate_b", [P, GH])
    mask8 = sb("mask8", [NS_TOK, NS_TOK])
    eps_col = sb("eps_col", [P, 1])
    v_st = sb("v_st", [P, 2, TOK])
    rank_z = sb("rank_z", [RANK, TOK])
    cum = sb("cum", [P, TOK])
    k_b = sb("k_b", [P, TOK])
    q_b = sb("q_b", [P, TOK])
    kd = sb("kd", [P, NP_TOK])
    kd_tok = sb("kd_tok", [P, 2, P])
    v_tok = sb("v_tok", [P, 2, GDV])
    ks_tok = sb("ks_tok", [NS_TOK, P])
    vs_tok = sb("vs_tok", [NS_TOK, GDV])
    k_diag = sb("k_diag", [NS_TOK, NS_TOK, P])
    lev = sb("lev", [P, LEVELS, 2, P])
    after_heads = lev[:].rearrange("c l s t -> c (l s t)")
    m_in = after_heads[:, 0:4 * TOK].rearrange("c (a b t) -> c a b t", a=2, b=2)
    merged = after_heads[:, 4 * TOK:6 * TOK].rearrange("c (a t) -> c a t", a=2)
    k_pad = sb("k_pad", [P, LEVELS - 1, NP_TOK])
    probs = sb("probs", [P, 2, CELLS])
    pairs = sb("pairs", [P, 3, P])
    S = sb("S", [P, 2, 4, GDV])
    s_out = sb("s_out", [P, GDV])
    sq = sb("sq", [P, 2, TOK])
    rs = sb("rs", [P, TOK])
    o_f = sb("o_f", [P, 2, TOK])

    bank = [ctx.enter_context(nc.psum_tensor(f"bank{i}", [P, 512], F32)) for i in range(8)]
    MM = bank[0:2]
    SC = bank[2:4]
    DG, TP = bank[4], bank[5]
    O = bank[6:8]

    slab_landed = [sem(f"slab_landed{i}") for i in range(RING)]
    hi_ready = sem("hi_ready")
    lo_ready = sem("lo_ready")
    slabs_multiplied = sem("slabs_multiplied")
    tiles_drained = sem("tiles_drained")
    x_landed = [sem(f"x_landed{i}") for i in range(4)]
    const_landed = sem("const_landed")
    consts_set = sem("consts_set")
    h_landed = sem("h_landed")
    a_hi_ready, a_lo_ready = sem("a_hi_ready"), sem("a_lo_ready")
    b_hi_ready, b_lo_ready = sem("b_hi_ready"), sem("b_lo_ready")
    squared, summed = sem("squared"), sem("summed")
    norm_sum_ready, root_ready, r_ready = sem("norm_sum_ready"), sem("root_ready"), sem("r_ready")
    gains_landed = sem("gains_landed")
    gates_ready, gates_stored = sem("gates_ready"), sem("gates_stored")
    silu_done = sem("silu_done")
    ls_abs, ls_exp, ls_ln = sem("ls_abs"), sem("ls_exp"), sem("ls_ln")
    ls_ready, gla_scaled, hk_log, hk_ready = sem("ls_ready"), sem("gla_scaled"), sem("hk_log"), sem("hk_ready")
    sample_gates, sums_ready = sem("sample_gates"), sem("sums_ready")
    stage_stored = [sem("stage_stored0"), sem("stage_stored1")]
    v_landed = sem("v_landed")
    s_landed = [sem("s_landed0"), sem("s_landed1")]
    s_stored = [sem("s_stored0"), sem("s_stored1")]
    state_stored = sem("state_stored")
    by_engine = {
        "act": ["v_tok_ready", "s_tok_ready", "lev_exp", "kd_exp", "kd_tok_ready", "sq_ready",
                "ln_rs", "rs_ready", "o_hi_done", "s_out_ready", "sg_abs", "sg_exp", "sg_ln", "sg_sigma"],
        "dve": ["lev_sub", "lev_ready", "kd_ready", "s_new0", "s_new1", "masked", "probs_ready", "sg_ls",
                "sg_ready", "o_scaled", "o_gated", "o_done"],
        "pe": ["v_turned", "s_turned", "outer0", "outer1", "so_done", "scores_done", "kd_turned",
               "pv_done", "state_done", "ss_done"],
        "pool": ["kq_ready", "k_diag_ready"],
    }
    h_sem = {n: sem(n) for names in by_engine.values() for n in names}
    m_landed = [sem("m_landed0"), sem("m_landed1")]
    sigma_ready, merge_ready = sem("sigma_ready"), sem("merge_ready")
    ht_ready, h_ready = sem("ht_ready"), sem("h_ready")
    u_ready = sem("u_ready")
    p_landed, p_hi_ready, p_lo_ready = sem("p_landed"), sem("p_hi_ready"), sem("p_lo_ready")
    pe_stored = sem("pe_stored")
    gate_pe, y_ready = sem("gate_pe"), sem("y_ready")
    y_stored = [sem("y_stored0"), sem("y_stored1")]

    def outer_at(D, r, i):
        if D == 1:
            return SC[r][:, i * P:(i + 1) * P]
        return (SC, O)[r][i // 2][:, (i % 2) * GDV:(i % 2 + 1) * GDV]

    PE_BANKS = [SC[0], SC[1], DG, O[0]]

    def now(H):
        return H + 2

    def before(H):
        return H + 1

    def tokens(ap, h, side):
        return ap.rearrange("c (p w j) -> c p w j", w=2, j=h)[:, :, side, :]

    def slot_of(par, half):
        return 2 * par + half

    def load_half(sp, T, par, half, first=False):
        s = slot_of(par, half)
        if not first:
            sp.wait_ge(lo_ready, 2 * T + (half - RING + 1))
        sp.dma_start(raw[:, s, :], t["stream"][T, :, half * SLAB:(half + 1) * SLAB]).then_inc(slab_landed[s], 16)

    def load(sp, T, par, first=False):
        for half in range(2):
            load_half(sp, T, par, half, first)

    def round_slab(act, T, par, half, first=False):
        s = slot_of(par, half)
        act.wait_ge(slab_landed[s], 8 * T + (16 - 8 * par))
        if not first:
            act.wait_ge(slabs_multiplied, 2 * T + (half - RING + 1))
        act.copy(whi[:, s, :], raw[:, s, :]).then_inc(hi_ready, 1)

    def rest_slab(dve, T, par, half):
        s = slot_of(par, half)
        dve.wait_ge(hi_ready, 2 * T + (half + 1))
        dve.tensor_tensor(wlo[:, s, :], raw[:, s, :], whi[:, s, :].bitcast(F32), ALU.subtract).then_inc(lo_ready, 1)

    def multiply(pe, T, par, half, out, hi, lo, k0, start, stop, before_k=None, midway=None):
        s = slot_of(par, half)
        pe.wait_ge(lo_ready, 2 * T + (half + 1))
        for k in range(HT):
            if before_k:
                before_k(k0 + k)
            if midway and k == HT // 2:
                midway()
            w = slice(k * P, (k + 1) * P)
            pe.matmul(out, whi[:, s, w], hi[:, k0 + k, :], start=start and k == 0, stop=False)
            pe.matmul(out, whi[:, s, w], lo[:, k0 + k, :], start=False, stop=False)
            mm = pe.matmul(out, wlo[:, s, w], hi[:, k0 + k, :], start=False, stop=stop and k == HT - 1)
        mm.then_inc(slabs_multiplied, 1)

    def tile(pe, T, par, hi, lo, first=False, before_half=None, before_k=None):
        if not first:
            pe.wait_ge(tiles_drained, T - 1)
        for half in range(2):
            if before_half:
                before_half(half)
            multiply(pe, T, par, half, MM[par][:, 0:TOK], hi, lo, half * HT, half == 0, half == 1, before_k)

    def tiles(eng, first, last, body):
        with eng.Fori(first, last, 2) as T:
            for j in range(2):
                body(T + j, (first + j) % 2)

    def tile_done(eng, T):
        eng.wait_ge(slabs_multiplied, 2 * T + 2)

    block = ctx.enter_context(nc.Block())

    @block.sync
    def _(sp):
        for i in range(4):
            sp.dma_start(x_in[:, 4 * i:4 * i + 4, :], t["x"][:, 4 * i:4 * i + 4, :]).then_inc(x_landed[i], 16)
            if i == 0:
                sp.dma_start(gains[:], t["gains"]).then_inc(gains_landed, 16)
            if i < 2:
                load(sp, i, i, first=True)
        for dst, name in ((masks, "masks"), (ident, "ident"), (head_gain, "head_gain"), (gate_w, "gate_w"),
                          (gate_b, "gate_b"), (mask8, "mask8")):
            sp.dma_start(dst[:], t[name]).then_inc(const_landed, 16)
        load(sp, 2, 0)
        tiles(sp, 3, T_HEADS + 1, lambda T, par: load(sp, T, par))

        def load_v(H, gla):
            v = t["v_spill"][:, bass.ds(2 * H - HH, 2) if gla else bass.ds(H, 1), :]
            sp.wait_ge(h_sem["s_turned"], before(H))
            sp.dma_start(v_st[:, 0:(2 if gla else 1), :], v).then_inc(v_landed, 16)

        def load_states(H, gla):
            sp.wait_ge(h_sem["so_done"], before(H))
            for r in range(2):
                sp.wait_ge(s_stored[r], 16 * H + 16)
                src = t["state_gla"][4 * r:4 * r + 4, H - HH] if gla else t["state_hgrn"][4 * r:4 * r + 4, H]
                w = GDV if gla else P
                sp.dma_start(S[:, r, :, 0:w], src.rearrange("b k v -> k b v")).then_inc(s_landed[r], 16)

        def head(H, gla, next_gla, more=True):
            T = 4 * H + T_HEADS
            h, w = (H - HH, GDV) if gla else (H, P)
            new = t["new_gla_sample" if gla else "new_hgrn_sample"]

            def m_spill(j):
                at = 2 * H + (HH + j - 2) if gla else 3 * H + (j - 1)
                par = (T_HEADS + j) % 2
                sp.wait_ge(tiles_drained, T + (j + 1))
                sp.dma_start(t["m_spill"][:, at, :], stage[:, par, :]).then_inc(stage_stored[par], 16)

            load(sp, T + 4, (T_HEADS + 4) % 2)
            load_half(sp, T + 5, (T_HEADS + 5) % 2, 0)
            for r in range(2):
                sp.wait_ge(h_sem[f"s_new{r}"], now(H))
                sp.dma_start(new[4 * r:4 * r + 4, h].rearrange("b k v -> k b v"), S[:, r, :, 0:w])\
                  .then_inc(s_stored[r], 16)
            load_half(sp, T + 5, (T_HEADS + 5) % 2, 1)
            if not gla:
                m_spill(1)
            if more:
                load_half(sp, T + 6, (T_HEADS + 6) % 2, 0)
                load_v(H + 1, next_gla)
                load_half(sp, T + 6, (T_HEADS + 6) % 2, 1)
                load_states(H + 1, next_gla)
            m_spill(2)
            if more:
                load(sp, T + 7, (T_HEADS + 7) % 2)
            sp.wait_ge(h_sem["s_out_ready"], now(H))
            sp.dma_start(t["new_gla_prompt" if gla else "new_hgrn_prompt"][h], s_out[:, 0:w])\
              .then_inc(state_stored, 16)
            m_spill(3)

        sp.wait_ge(stage_stored[0], 16 * (1 + HH))
        sp.wait_ge(stage_stored[1], 16 * (1 + HH))
        load_v(0, False)
        load_states(0, False)
        tiles(sp, T_HEADS + 2, T_HEADS + 3, lambda T, par: load(sp, T, par))
        with sp.Fori(0, HH - 1) as H:
            head(H, False, False)
        with sp.Fori(HH - 1, HH) as H:
            head(H, False, True)
        with sp.Fori(HH, HEADS - 1) as H:
            head(H, True, True)
        with sp.Fori(HEADS - 1, HEADS) as H:
            head(H, True, None, more=False)

        sp.wait_ge(stage_stored[0], 16 * (1 + HH + 2 * HH + GH))
        sp.wait_ge(stage_stored[1], 16 * (1 + HH + HH + GH))

        def up_loads(T, par):
            load(sp, T + 2, par)
            sp.wait_ge(merge_ready, T - T_UP + 1)
            sp.dma_start(m_in[:, par_of_m(par), :, :], t["m_spill"][:, bass.ds(2 * (T - T_UP), 2), :])\
              .then_inc(m_landed[par_of_m(par)], 16)

        def par_of_m(par):
            return (par - T_UP) % 2

        tiles(sp, T_UP, T_OUT - 1, up_loads)
        sp.wait_ge(h_sem["o_done"], now(HEADS - 1))
        for i in range(4):
            sp.dma_start(h_res[:, 4 * i:4 * i + 4, :], t["x"][:, 4 * i:4 * i + 4, :]).then_inc(h_landed, 16)
        sp.dma_start(stage[:], t["p"]).then_inc(p_landed, 16)
        tiles(sp, T_OUT + 2, T_GATE + 1, lambda T, par: load(sp, T, par))
        load(sp, T_GATE + 2, T_GATE % 2)

        def store_y(T, par):
            j = (par - T_GATE) % 2
            sp.wait_ge(y_ready, T - T_GATE + 3)
            sp.dma_start(t["y"][:, T - T_GATE, :], merged[:, j, :]).then_inc(y_stored[j], 16)

        def load_and_store(T, par):
            load(sp, T + 3, 1 - par)
            store_y(T, par)

        tiles(sp, T_GATE, T_END - 5, load_and_store)
        load(sp, T_END - 1, (T_END - 1) % 2)
        for T in range(T_END - 4, T_END):
            store_y(T, T % 2)
        for j in range(2):
            sp.wait_ge(y_stored[j], 16 + 16 * KT // 2)
        for r in range(2):
            sp.wait_ge(s_stored[r], 16 * (HEADS + 1))
        sp.wait_ge(state_stored, 16 * (HEADS + 1))

    @block.tensor
    def _(pe):
        for n in by_engine["pe"]:
            pe.sem_inc(h_sem[n], 1)

        tile(pe, T_RANK, 0, a_hi, a_lo, first=True, before_k=lambda k: pe.wait_ge(a_lo_ready, k + 1))
        pe.wait_ge(consts_set, 1)
        pe.wait_ge(summed, KT)
        pe.matmul(TP[:, 0:TOK], ones[:], sq[:, 1, :], start=True, stop=True).then_inc(norm_sum_ready, 1)
        tile(pe, T_F, 1, a_hi, a_lo, first=True)
        pe.wait_ge(tiles_drained, 1)
        pe.wait_ge(const_landed, 16 * 6)
        for h in range(GH):
            mm = pe.matmul(PE_BANKS[h][:, 0:TOK], gate_w[:, h * P:(h + 1) * P], rank_z[:],
                           start=True, stop=True)
        mm.then_inc(gates_ready, 1)
        tile(pe, T_F + 1, 0, a_hi, a_lo)
        tiles(pe, T_F + 2, T_HEADS - 1, lambda T, par: tile(pe, T, par, a_hi, a_lo))

        def turn_v(H, D):
            pe.wait_ge(v_landed, 16 * H + 16)
            pe.wait_ge(h_sem["s_out_ready"], before(H))
            for B in range(2):
                for d in range(D):
                    mm = pe.transpose(TP[:, (B * D + d) * P:(B * D + d + 1) * P], v_st[:, d, B * P:(B + 1) * P],
                                      ident[:, 0:P])
            mm.then_inc(h_sem["v_turned"], 1)

        def turn_s(H, D):
            pe.wait_ge(h_sem["kq_ready"], now(H))
            pe.wait_ge(h_sem["probs_ready"], before(H))
            pe.transpose(SC[1][0:NS_TOK, 0:P], k_b[:, NP_TOK:TOK], ident[:, 0:P])
            for d in range(D):
                mm = pe.transpose(SC[1][0:NS_TOK, (1 + d) * P:(2 + d) * P], v_st[:, d, NP_TOK:TOK], ident[:, 0:P])
            mm.then_inc(h_sem["s_turned"], 1)

        def outer(H, D, r):
            if r == 0:
                pe.wait_ge(h_sem["k_diag_ready"], now(H))
                pe.wait_ge(h_sem["s_tok_ready"], now(H))
            elif D == 2:
                pe.wait_ge(h_sem["o_scaled"], before(H))
            for i in range(4):
                mm = pe.matmul(outer_at(D, r, i), k_diag[:, 4 * r + i, :], vs_tok[:, 0:D * P], start=True, stop=True)
            mm.then_inc(h_sem[f"outer{r}"], 1)

        def sample_out(H, D, r):
            pe.wait_ge(h_sem["o_scaled"], before(H))
            pe.wait_ge(h_sem["s_new1" if D == 2 else f"s_new{r}"], now(H))
            for i in range(4):
                for d in range(D):
                    b = NP_TOK + 4 * r + i
                    mm = pe.matmul(O[d][:, b:b + 1], S[:, r, i, d * P:(d + 1) * P], q_b[:, b:b + 1],
                                   start=(r == 0 and i == 0), stop=True, skip_group_check=True)
            if r == 1:
                mm.then_inc(h_sem["so_done"], 1)

        def scores(H, D):
            pe.wait_ge(h_sem["lev_ready"], now(H))
            pe.wait_ge(h_sem["s_new1"], now(H))
            pe.wait_ge(h_sem["ln_rs"], before(H))
            for B in range(2):
                at = slice(B * P, (B + 1) * P)
                pe.matmul(DG[:, 2 * B * P:(2 * B + 1) * P], k_b[:, at], q_b[:, at], start=True, stop=True)
                for l in range(1, LEVELS):
                    pe.matmul(SC[B][:, (l - 1) * 64:l * 64], k_pad[:, l - 1, at], lev[:, l, 0, B * 64:(B + 1) * 64],
                              start=True, stop=True)
            pe.matmul(DG[:, P:2 * P], lev[:, 0, 1, :], lev[:, 0, 0, :], start=True, stop=True)\
              .then_inc(h_sem["scores_done"], 1)

        def turn_kd(H):
            pe.wait_ge(h_sem["kd_ready"], now(H))
            pe.wait_ge(h_sem["v_tok_ready"], now(H))
            for B in range(2):
                mm = pe.transpose(TP[:, B * P:(B + 1) * P], kd[:, B * P:(B + 1) * P], ident[:, 0:P])
            mm.then_inc(h_sem["kd_turned"], 1)

        def prob_v(H, D):
            pe.wait_ge(h_sem["probs_ready"], now(H))
            for d in range(D):
                v = slice(d * P, (d + 1) * P)
                pe.matmul(O[d][:, 0:2 * P], v_tok[:, 0, v], pairs[:, 0:2, :], start=False, stop=False, skip_group_check=True)
                mm = pe.matmul(O[d][:, P:2 * P], v_tok[:, 1, v], pairs[:, 2, :], start=False, stop=True, skip_group_check=True)
            mm.then_inc(h_sem["pv_done"], 1)

        def state(H, D):
            pe.wait_ge(h_sem["kd_tok_ready"], now(H))
            for B in range(2):
                mm = pe.matmul(TP[:, 0:D * P], kd_tok[:, B, :], v_tok[:, B, 0:D * P], start=B == 0, stop=B == 1)
            mm.then_inc(h_sem["state_done"], 1)

        def head_norm(H, D):
            pe.wait_ge(h_sem["sq_ready"], now(H))
            for d in range(D):
                mm = pe.matmul(DG[:, 0:TOK], ones[:], sq[:, d, :], start=d == 0, stop=d == D - 1)
            mm.then_inc(h_sem["ss_done"], 1)

        def head(H, D):
            T = 4 * H + T_HEADS

            def slab(k, midway=None):
                j, half = k // 2, k % 2
                par = (T_HEADS + j) % 2
                if half == 0:
                    pe.wait_ge(tiles_drained, T + (j - 1))
                multiply(pe, T + j, par, half, MM[par][:, 0:TOK], a_hi, a_lo, half * HT, half == 0, half == 1, midway=midway)

            slab(0)
            turn_v(H, D)
            turn_s(H, D)
            slab(1)
            slab(2)
            slab(3, midway=lambda: outer(H, D, 0))
            outer(H, D, 1)
            slab(4, midway=lambda: turn_kd(H))
            sample_out(H, D, 0)
            slab(5, midway=lambda: scores(H, D))
            sample_out(H, D, 1)
            slab(6)
            prob_v(H, D)

            def norm_and_state():
                head_norm(H, D)
                state(H, D)

            slab(7, midway=norm_and_state)

        with pe.Fori(0, HH) as H:
            head(H, 1)
        with pe.Fori(HH, HEADS) as H:
            head(H, 2)

        pe.wait_ge(h_sem["o_done"], now(HH - 1))

        def up(T, par):
            pe.wait_ge(tiles_drained, T - 1)
            multiply(pe, T, par, 0, MM[par][:, 0:TOK], b_hi, b_lo, 0, True, True)
            pe.wait_ge(h_sem["o_done"], now(HEADS - 1))
            multiply(pe, T, par, 1, SC[par][:, 0:TOK], b_hi, b_lo, HT, True, True)

        tiles(pe, T_UP, T_OUT - 1, up)

        def out_proj(T, par):
            tile(pe, T, par, a_hi, a_lo, before_half=lambda half: pe.wait_ge(a_lo_ready, KT + HT * (half + 1)))

        tiles(pe, T_OUT, T_FF - 1, out_proj)

        def norm_sum(n):
            pe.wait_ge(summed, KT * (n + 1))
            pe.matmul(TP[:, 0:TOK], ones[:], sq[:, 1, :], start=True, stop=True).then_inc(norm_sum_ready, 1)

        norm_sum(1)
        for j in range(FF_BLOCKS):
            T0 = T_FF + 2 * KT * j
            if j == 0:
                tile(pe, T0, T0 % 2, b_hi, b_lo, before_k=lambda k: pe.wait_ge(b_lo_ready, k + 1))
                norm_sum(2)
                tile(pe, T0 + 1, (T0 + 1) % 2, b_hi, b_lo)
            tiles(pe, T0 + 2 * (j == 0), T0 + KT - 1, lambda T, par: tile(pe, T, par, b_hi, b_lo))
            tiles(pe, T0 + KT, T0 + 2 * KT - 1, lambda T, par: tile(
                pe, T, par, a_hi, a_lo,
                before_half=lambda half: pe.wait_ge(a_lo_ready, KT * (2 + j) + HT * (half + 1))))

        norm_sum(3)
        pe.wait_ge(p_lo_ready, 1)
        for i in range(4):
            T, half = T_PLE + i // 2, i % 2
            s = slot_of(T % 2, half)
            pe.wait_ge(lo_ready, 2 * T + half + 1)
            for o in range(4):
                if i >= 1:
                    pe.wait_ge(pe_stored, 4 * (i - 1) + o + 1)
                out = PE_BANKS[o][:, 0:TOK]
                for k in range(2):
                    w = slice((2 * o + k) * P, (2 * o + k + 1) * P)
                    pe.matmul(out, whi[:, s, w], p_hi[:, k, :], start=k == 0, stop=False)
                    pe.matmul(out, whi[:, s, w], p_lo[:, k, :], start=False, stop=False)
                    mm = pe.matmul(out, wlo[:, s, w], p_hi[:, k, :], start=False, stop=k == 1)
            mm.then_inc(slabs_multiplied, 1)
        pe.wait_ge(tiles_drained, T_PLE)
        for j in range(2):
            T = T_GATE + j
            tile(pe, T, T % 2, b_hi, b_lo, first=True, before_k=(lambda k: pe.wait_ge(b_lo_ready, KT + k + 1)) if j == 0 else None)
        tiles(pe, T_GATE + 2, T_END - 1, lambda T, par: tile(pe, T, par, b_hi, b_lo))

    @block.scalar
    def _(act):
        for n in by_engine["act"]:
            act.sem_inc(h_sem[n], 1)
        for s in (*stage_stored, *s_stored, state_stored):
            act.sem_inc(s, 16)

        def split(T, par):
            for half in range(2):
                round_slab(act, T, par, half)

        act.wait_ge(gains_landed, 16)
        for k in range(KT):
            if k % 4 == 0:
                act.wait_ge(x_landed[k // 4], 16)
            if k in (4, 8):
                round_slab(act, 0, 0, k // 4 - 1, first=True)
            act.activation(a_hi[:, k, :], x_in[:, k, :], ACT.Identity, scale=gains[:, 0, k:k + 1]).then_inc(a_hi_ready, 1)
        for half in range(2):
            round_slab(act, 1, 1, half, first=True)

        def root(n):
            act.wait_ge(norm_sum_ready, n + 1)
            act.activation(rs[:], TP[:, 0:TOK], ACT.Sqrt, scale=1.0 / D_MODEL, bias=eps_col[:]).then_inc(root_ready, 1)

        act.wait_ge(consts_set, 1)
        root(0)
        split(2, 0)
        act.wait_ge(gates_ready, 1)
        for h in range(GH):
            src = PE_BANKS[h][:, 0:TOK]
            act.activation(zf[:, HH + h, :], src, ACT.Identity, bias=gate_b[:, h:h + 1]).then_inc(gates_stored, 1)
        split(3, 1)
        tiles(act, T_F + 2, T_Q - 1, lambda T, par: split(T + 1, 1 - par))

        def q_tile(T, par):
            split(T + 1, 1 - par)
            act.wait_ge(tiles_drained, T + 1)
            act.activation(zq[:, T - T_Q, :], stage[:, par, :], ACT.Silu).then_inc(silu_done, 1)

        tiles(act, T_Q, T_GQ - 1, q_tile)

        for T in range(T_GQ, T_V):
            split(T + 1, 1 - T % 2)
            if T == T_GQ:
                act.wait_ge(tiles_drained, T_Q)
                act.wait_ge(gates_stored, GH)
                act.activation(log_gate, zf, ACT.Abs).then_inc(ls_abs, 1)
            elif T == T_GQ + 1:
                act.wait_ge(ls_abs, 1)
                act.activation(log_gate, log_gate, ACT.Exp, scale=-1.0).then_inc(ls_exp, 1)
            elif T == T_GQ + 2:
                act.wait_ge(ls_exp, 1)
                act.activation(log_gate, log_gate, ACT.Ln, bias=ones[:, 0:1]).then_inc(ls_ln, 1)
            elif T == T_GQ + 5:
                act.wait_ge(hk_log, 1)
                act.activation(hk, hk, ACT.Exp).then_inc(hk_ready, 1)
                act.wait_ge(gla_scaled, 1)
                act.activation(gates[:, :, NP_TOK:TOK], log_gate[:, :, NP_TOK:TOK], ACT.Exp).then_inc(sample_gates, 1)

        def spill(T, par, to, at):
            act.wait_ge(tiles_drained, T + 1)
            act.dma_start(t[to][:, at, :], stage[:, par, :]).then_inc(stage_stored[par], 16)

        def v_tile(T, par):
            split(T + 1, 1 - par)
            spill(T, par, "v_spill", T - T_V)

        tiles(act, T_V, T_HEADS - 1, v_tile)

        act.wait_ge(tiles_drained, T_V)
        act.wait_ge(silu_done, 2 + HH)

        def head(H, D, more=True):
            T = 4 * H + T_HEADS

            def slab(k):
                round_slab(act, T + (1 + k // 2), (T_HEADS + 1 + k // 2) % 2, k % 2)

            def exp_gate():
                act.wait_ge(tiles_drained, T + D)
                act.wait_ge(h_sem["sg_ready"], before(H))
                e = sgl[:, 0:D, :]
                act.activation(e, sgz[:, 0:D, :], ACT.Abs).then_inc(h_sem["sg_abs"], 1)
                act.wait_ge(h_sem["sg_abs"], now(H))
                act.activation(e, e, ACT.Exp, scale=-1.0).then_inc(h_sem["sg_exp"], 1)

            slab(2)
            act.wait_ge(h_sem["s_turned"], now(H))
            act.wait_ge(h_sem["outer1"], before(H))
            act.copy(ks_tok[:], SC[1][0:NS_TOK, 0:P])
            act.copy(vs_tok[:, 0:D * P], SC[1][0:NS_TOK, P:(1 + D) * P]).then_inc(h_sem["s_tok_ready"], 1)
            act.wait_ge(h_sem["lev_sub"], now(H))
            act.activation(lev[:], lev[:], ACT.Exp).then_inc(h_sem["lev_exp"], 1)
            act.wait_ge(h_sem["kq_ready"], now(H))
            act.wait_ge(h_sem["kd_turned"], before(H))
            act.activation(kd[:], cum[:, 0:NP_TOK], ACT.Exp, scale=-1.0, bias=cum[:, NP_TOK - 1:NP_TOK])\
               .then_inc(h_sem["kd_exp"], 1)
            act.wait_ge(h_sem["v_turned"], now(H))
            act.wait_ge(h_sem["state_done"], before(H))
            act.copy(v_tok[:, :, 0:D * P], TP[:, 0:2 * D * P].rearrange("s (b v) -> s b v", b=2))\
               .then_inc(h_sem["v_tok_ready"], 1)
            slab(3)
            slab(4)
            if D == 1:
                exp_gate()
            slab(5)
            act.wait_ge(h_sem["kd_turned"], now(H))
            act.copy(kd_tok[:], TP[:, 0:2 * P].rearrange("s (b k) -> s b k", b=2)).then_inc(h_sem["kd_tok_ready"], 1)
            slab(6)
            if D == 2:
                exp_gate()
            slab(7)
            act.wait_ge(h_sem["pv_done"], now(H))
            act.wait_ge(h_sem["ss_done"], before(H))
            for d in range(D):
                sqd = act.activation(sq[:, d, :], O[d][:, 0:TOK], ACT.Square)
            sqd.then_inc(h_sem["sq_ready"], 1)
            if more:
                slab(8)
            act.wait_ge(h_sem["sg_exp"], now(H))
            act.activation(sgl[:, 0:D, :], sgl[:, 0:D, :], ACT.Ln, bias=ones[:, 0:1]).then_inc(h_sem["sg_ln"], 1)
            act.wait_ge(h_sem["ss_done"], now(H))
            act.wait_ge(h_sem["probs_ready"], now(H))
            act.wait_ge(h_sem["o_scaled"], before(H))
            act.activation(rs[:], DG[:, 0:TOK], ACT.Ln, scale=1.0 / (D * P), bias=eps_col[:])\
               .then_inc(h_sem["ln_rs"], 1)
            act.wait_ge(h_sem["state_done"], now(H))
            act.wait_ge(state_stored, 16 * H + 16)
            act.copy(s_out[:, 0:D * P], TP[:, 0:D * P]).then_inc(h_sem["s_out_ready"], 1)
            act.wait_ge(h_sem["ln_rs"], now(H))
            act.activation(rs[:], rs[:], ACT.Exp, scale=-0.5).then_inc(h_sem["rs_ready"], 1)
            act.wait_ge(h_sem["sg_ls"], now(H))
            act.activation(sgl[:, 0:D, :], sgl[:, 0:D, :], ACT.Exp).then_inc(h_sem["sg_sigma"], 1)
            if more:
                slab(9)
            act.wait_ge(h_sem["o_gated"], now(H))
            k = H if D == 1 else 2 * H - HH
            act.copy(b_hi[:, bass.ds(k, D), :], o_f[:, 0:D, :]).then_inc(h_sem["o_hi_done"], 1)

        split(T_HEADS + 1, (T_HEADS + 1) % 2)
        with act.Fori(0, HH) as H:
            head(H, 1)
        with act.Fori(HH, HEADS - 1) as H:
            head(H, 2)
        with act.Fori(HEADS - 1, HEADS) as H:
            head(H, 2, more=False)

        def merged_hi(n, m):
            act.wait_ge(merge_ready, n + 3)
            act.copy(a_hi[:, n, :], merged[:, m, :]).then_inc(a_hi_ready, 1)

        def merge(T, par, first=False):
            m = (par - T_UP) % 2
            split(T + 1, 1 - par)
            act.wait_ge(m_landed[m], 8 * (T - T_UP) + (16 - 8 * m))
            act.activation(m_in[:, m, :, :], m_in[:, m, :, :], ACT.Sigmoid).then_inc(sigma_ready, 1)
            if not first:
                merged_hi(T - T_UP - 1, 1 - m)

        merge(T_UP, T_UP % 2, first=True)
        merge(T_UP + 1, 1 - T_UP % 2)
        tiles(act, T_UP + 2, T_OUT - 1, merge)
        merged_hi(KT - 1, 1)
        tiles(act, T_OUT, T_FF - 1, lambda T, par: split(T + 1, 1 - par))

        root(1)
        for k in range(KT):
            act.wait_ge(h_ready, k + 1)
            act.activation(b_hi[:, k, :], h_res[:, k, :], ACT.Identity, scale=gains[:, 2, k:k + 1])\
               .then_inc(b_hi_ready, 1)
        root(2)

        for j in range(FF_BLOCKS):
            T0 = T_FF + 2 * KT * j

            def ff1(T, par):
                split(T + 1, 1 - par)
                i = KT * j + T - T0
                act.wait_ge(tiles_drained, T + 1)
                act.activation(merged[:, par, :], merged[:, par, :], ACT.Square).then_inc(u_ready, 1)
                act.wait_ge(u_ready, i + 1)
                act.copy(a_hi[:, T - T0, :], merged[:, par, :]).then_inc(a_hi_ready, 1)

            tiles(act, T0, T0 + KT - 1, ff1)
            tiles(act, T0 + KT, T0 + 2 * KT - 1, lambda T, par: split(T + 1, 1 - par))

        split(T_PLE + 1, (T_PLE + 1) % 2)
        act.wait_ge(p_landed, 16)
        act.wait_ge(slabs_multiplied, 2 * T_PLE)
        act.copy(p_hi, stage[:]).then_inc(p_hi_ready, 1)
        root(3)
        for k in range(KT):
            act.wait_ge(h_ready, KT + k + 1)
            act.copy(b_hi[:, k, :], h_res[:, k, :]).then_inc(b_hi_ready, 1)
            act.wait_ge(slabs_multiplied, 2 * T_PLE + k // 4 + 1)
            act.copy(t_acc[:, k, :], PE_BANKS[k % 4][:, 0:TOK]).then_inc(pe_stored, 1)
            if k == 7:
                split(T_GATE, T_GATE % 2)
        act.sem_inc(tiles_drained, 2)

        def gate(T, par, last=False):
            if not last:
                split(T + 1, 1 - par)
            tile_done(act, T)
            act.wait_ge(y_ready, T - T_GATE + 1)
            act.activation(sq[:, par, :], MM[par][:, 0:TOK], ACT.Sigmoid).then_inc(tiles_drained, 1)

        tiles(act, T_GATE, T_END - 3, gate)
        gate(T_END - 2, (T_END - 2) % 2)
        gate(T_END - 1, (T_END - 1) % 2, last=True)

    @block.vector
    def _(dve):
        for n in by_engine["dve"]:
            dve.sem_inc(h_sem[n], 1)
        dve.sem_inc(merge_ready, 2)
        dve.sem_inc(y_ready, 2)
        dve.sem_inc(silu_done, 2)

        def split(T, par):
            for half in range(2):
                rest_slab(dve, T, par, half)

        def gained_rest(k, hi, lo, src, gain, ready, done, base=0):
            dve.wait_ge(ready, base + k + 1)
            dve.scalar_tensor_tensor(out=lo[:, k, :], in0=src[:, k, :], scalar=gain, in1=hi[:, k, :].bitcast(F32),
                                     op0=ALU.mult, op1=ALU.subtract).then_inc(done, 1)

        for k in range(KT):
            if k in (4, 8):
                rest_slab(dve, 0, 0, k // 4 - 1)
            gained_rest(k, a_hi, a_lo, x_in, gains[:, 0, k:k + 1], a_hi_ready, a_lo_ready)
        split(1, 1)

        def invert(n):
            dve.wait_ge(root_ready, n + 1)
            dve.reciprocal(r_bc[:], rs[:]).then_inc(r_ready, 1)
            dve.wait_ge(r_ready, n + 1)

        def drain(T, par, out, scale=None, rows=P):
            tile_done(dve, T)
            src = MM[par][0:rows, 0:TOK]
            if scale is None:
                return dve.tensor_tensor(out, src, r_bc[0:rows, :], ALU.mult)
            return dve.scalar_tensor_tensor(out=out, in0=src, scalar=scale, in1=r_bc[:], op0=ALU.mult, op1=ALU.mult)

        invert(0)
        drain(0, 0, rank_z[:], rows=RANK).then_inc(tiles_drained, 1)
        split(2, 0)
        drain(T_F, 1, zf[:, 0, :]).then_inc(tiles_drained, 1)
        split(3, 1)
        drain(T_F + 1, 0, zf[:, 1, :]).then_inc(tiles_drained, 1)

        def stored(base, dst, scale=None):
            def body(T, par):
                split(T + 1, 1 - par)
                drain(T, par, dst[:, T - base, :], scale).then_inc(tiles_drained, 1)
            return body

        tiles(dve, T_F + 2, T_Q - 1, stored(T_F, zf))

        def q_tile(T, par):
            split(T + 1, 1 - par)
            dve.wait_ge(silu_done, T - T_Q + 1)
            drain(T, par, stage[:, par, :]).then_inc(tiles_drained, 1)

        tiles(dve, T_Q, T_GQ - 1, q_tile)

        def sums(first, last):
            for H in range(first, last):
                dve.tensor_tensor_scan(gates[:, H, 0:NP_TOK], ones[:, 0:1].to_broadcast([P, NP_TOK]),
                                       log_gate[:, H, 0:NP_TOK], 0.0, ALU.mult, ALU.add).then_inc(sums_ready, 1)

        for T in range(T_GQ, T_V):
            (stored(T_GQ - HH, zq, P ** -0.5) if T < T_GK else stored(T_GK, zk))(T, T % 2)
            if T == T_GQ + 3:
                dve.wait_ge(ls_ln, 1)
                dve.scalar_tensor_tensor(out=log_gate, in0=zf, scalar=0.0, in1=log_gate, op0=ALU.min,
                                         op1=ALU.subtract).then_inc(ls_ready, 1)
            elif T == T_GQ + 4:
                dve.wait_ge(ls_ready, 1)
                dve.tensor_tensor(hk, log_gate[:, 0:HH, :], zf[:, 0:HH, :], ALU.subtract).then_inc(hk_log, 1)
                gla = log_gate[:, HH:HEADS, :]
                dve.tensor_scalar(gla, gla, 1.0 / GATE_NORM, None, ALU.mult).then_inc(gla_scaled, 1)
            elif T == T_GQ + 5:
                dve.wait_ge(gla_scaled, 1)
                dve.wait_ge(hk_log, 1)
                sums(0, 4)
            elif T == T_GQ + 6:
                sums(4, 8)
            elif T == T_GQ + 7:
                sums(8, HEADS)
        dve.wait_ge(silu_done, 2 + HH)

        def to_stage(T, par, uses):
            dve.wait_ge(stage_stored[par], 16 * uses + 16)
            drain(T, par, stage[:, par, :]).then_inc(tiles_drained, 1)

        with dve.Fori(0, HH) as i:
            for j in range(2):
                T = 2 * i + (T_V + j)
                par = (T_V + j) % 2
                split(T + 1, 1 - par)
                to_stage(T, par, i)

        dve.wait_ge(gates_stored, GH)
        dve.wait_ge(const_landed, 16 * 6)

        def level_decays(l):
            h = HALF[l]
            pairs = P // h
            left, right = tokens(cum[:, 0:NP_TOK], h, 0), tokens(cum[:, 0:NP_TOK], h, 1)
            mid = left[:, :, h - 1:h].to_broadcast([P, pairs, h])
            dve.tensor_tensor(lev[:, l, 0, :].rearrange("c (p j) -> c p j", j=h), right, mid, ALU.subtract)
            return dve.tensor_tensor(lev[:, l, 1, :].rearrange("c (p j) -> c p j", j=h), mid, left, ALU.subtract)

        def level_half(second):
            for l in range(LEVELS // 2 * second, LEVELS // 2 * (1 + second)):
                last = level_decays(l)
            if second:
                last.then_inc(h_sem["lev_sub"], 1)

        dve.wait_ge(h_sem["kq_ready"], now(0))
        level_half(0)
        level_half(1)

        def head(H, D, more=True):
            T = 4 * H + T_HEADS

            def slab(k):
                rest_slab(dve, T + (1 + k // 2), (T_HEADS + 1 + k // 2) % 2, k % 2)

            def m_tile(j):
                par = (T_HEADS + j) % 2
                if D == 1:
                    uses = H + HH if par else 2 * H + (HH + (j == 3))
                else:
                    uses = H + HH if par else H + 2 * HH
                to_stage(T + j, par, uses)

            def gate_tile(d):
                last = drain(T + d, (T_HEADS + d) % 2, sgz[:, d, :])
                last.then_inc(tiles_drained, 1)

            def new_states(r):
                dve.wait_ge(s_landed[r], 16 * H + 16)
                dve.wait_ge(h_sem[f"outer{r}"], now(H))
                for i in range(4):
                    s, b = S[:, r, i, 0:D * P], NP_TOK + 4 * r + i
                    last = dve.scalar_tensor_tensor(out=s, in0=s, scalar=cum[:, b:b + 1], in1=outer_at(D, r, i),
                                                    op0=ALU.mult, op1=ALU.add)
                last.then_inc(h_sem[f"s_new{r}"], 1)

            def level_operands(l):
                h = HALF[l]
                q, k = tokens(q_b[:, 0:NP_TOK], h, 1), tokens(k_b[:, 0:NP_TOK], h, 0)
                lq = lev[:, l, 0, :].rearrange("c (p j) -> c p j", j=h)
                lk = lev[:, l, 1, :].rearrange("c (p j) -> c p j", j=h)
                dve.tensor_tensor(lq, lq, q, ALU.mult)
                return dve.tensor_tensor(lk if l == 0 else tokens(k_pad[:, l - 1, :], h, 0), lk, k, ALU.mult)

            slab(2)
            dve.wait_ge(h_sem["lev_exp"], now(H))
            for l in range(LEVELS // 2):
                level_operands(l)
            slab(3)
            gate_tile(0)
            for l in range(LEVELS // 2, LEVELS):
                last = level_operands(l)
            last.then_inc(h_sem["lev_ready"], 1)
            dve.wait_ge(h_sem["kd_exp"], now(H))
            dve.tensor_tensor(kd[:], kd[:], k_b[:, 0:NP_TOK], ALU.mult).then_inc(h_sem["kd_ready"], 1)
            slab(4)
            new_states(0)
            new_states(1)
            slab(5)
            if D == 1:
                m_tile(1)
            else:
                gate_tile(1)
            slab(6)
            dve.wait_ge(h_sem["scores_done"], now(H))
            dve.wait_ge(h_sem["pv_done"], before(H))
            for B in range(2):
                dve.tensor_tensor(probs[:, B, :], SC[B][:, 0:CELLS], masks[:], ALU.mult).then_inc(h_sem["masked"], 1)
            dve.tensor_tensor(pairs[:], DG[:, 0:3 * P].rearrange("s (b t) -> s b t", b=3),
                              ident[:].rearrange("s (b t) -> s b t", b=3), ALU.mult).then_inc(h_sem["masked"], 1)
            for l in range(1, LEVELS):
                h = HALF[l]
                to = pairs[:, 0:3:2, :].rearrange("s b (p w j) -> s b p w j", w=2, j=h)[:, :, :, 1, :]
                cells = probs[:, :, (l - 1) * 64:l * 64].rearrange("s b (p j) -> s b p j", j=h)
                dve.wait_ge(h_sem["masked"], (LEVELS + 1) * H + (l + 3))
                last = dve.tensor_tensor(to, to, cells, ALU.add)
                last.then_inc(h_sem["probs_ready" if l == LEVELS - 1 else "masked"], 1)
            slab(7)
            m_tile(2)
            if more:
                slab(8)
            z, e = sgz[:, 0:D, :], sgl[:, 0:D, :]
            dve.wait_ge(h_sem["sg_ln"], now(H))
            dve.scalar_tensor_tensor(out=e, in0=z, scalar=0.0, in1=e, op0=ALU.min, op1=ALU.subtract)\
               .then_inc(h_sem["sg_ls"], 1)
            if more:
                dve.wait_ge(h_sem["kq_ready"], now(H + 1))
                level_half(0)
                slab(9)
            m_tile(3)
            dve.wait_ge(h_sem["sg_sigma"], now(H))
            dve.tensor_tensor(z, z, e, ALU.mult).then_inc(h_sem["sg_ready"], 1)
            dve.wait_ge(h_sem["rs_ready"], now(H))
            dve.wait_ge(h_sem["o_hi_done"], before(H))
            for d in range(D):
                gain = head_gain[:, (0 if D == 1 else 1 + d):(1 if D == 1 else 2 + d)]
                last = dve.scalar_tensor_tensor(out=o_f[:, d, :], in0=O[d][:, 0:TOK], scalar=gain, in1=rs[:],
                                                op0=ALU.mult, op1=ALU.mult)
            last.then_inc(h_sem["o_scaled"], 1)
            dve.wait_ge(h_sem["o_scaled"], now(H))
            dve.wait_ge(h_sem["sg_ready"], now(H))
            dve.tensor_tensor(o_f[:, 0:D, :], o_f[:, 0:D, :], sgz[:, 0:D, :], ALU.mult).then_inc(h_sem["o_gated"], 1)
            if more:
                level_half(1)
            dve.wait_ge(h_sem["o_hi_done"], now(H))
            k = H if D == 1 else 2 * H - HH
            dve.tensor_tensor(b_lo[:, bass.ds(k, D), :], o_f[:, 0:D, :], b_hi[:, bass.ds(k, D), :].bitcast(F32),
                              ALU.subtract).then_inc(h_sem["o_done"], 1)

        split(T_HEADS + 1, (T_HEADS + 1) % 2)
        with dve.Fori(0, HH) as H:
            head(H, 1)
        with dve.Fori(HH, HEADS - 1) as H:
            head(H, 2)
        with dve.Fori(HEADS - 1, HEADS) as H:
            head(H, 2, more=False)

        def merged_lo(n, m):
            dve.wait_ge(a_hi_ready, n + (KT + 1))
            dve.tensor_tensor(a_lo[:, n, :], merged[:, m, :], a_hi[:, n, :].bitcast(F32), ALU.subtract)\
               .then_inc(a_lo_ready, 1)

        def merge(T, par, first=False):
            split(T + 1, 1 - par)
            n, m = T - T_UP, (par - T_UP) % 2
            if not first:
                merged_lo(n - 1, 1 - m)
            tile_done(dve, T)
            dve.wait_ge(sigma_ready, n + 1)
            dve.tensor_tensor(m_in[:, m, 0, :], m_in[:, m, 0, :], MM[par][:, 0:TOK], ALU.mult)
            dve.tensor_tensor(m_in[:, m, 1, :], m_in[:, m, 1, :], SC[par][:, 0:TOK], ALU.mult).then_inc(tiles_drained, 1)
            dve.wait_ge(tiles_drained, T + 1)
            dve.tensor_tensor(merged[:, m, :], m_in[:, m, 0, :], m_in[:, m, 1, :], ALU.add).then_inc(merge_ready, 1)

        merge(T_UP, T_UP % 2, first=True)
        merge(T_UP + 1, 1 - T_UP % 2)
        tiles(dve, T_UP + 2, T_OUT - 1, merge)
        merged_lo(KT - 1, 1)

        def keep_t(T0, add):
            def body(T, par):
                split(T + 1, 1 - par)
                tile_done(dve, T)
                out = t_acc[:, T - T0, :]
                if add:
                    ins = dve.tensor_tensor(out, out, MM[par][:, 0:TOK], ALU.add)
                else:
                    ins = dve.tensor_copy(out, MM[par][:, 0:TOK])
                ins.then_inc(tiles_drained, 1)
            return body

        tiles(dve, T_OUT, T_FF - 1, keep_t(T_OUT, False))

        def residual(norm, gain_at, gain_next, count):
            for k in range(KT):
                dve.scalar_tensor_tensor(out=t_acc[:, k, :], in0=t_acc[:, k, :], scalar=gains[:, gain_at, k:k + 1],
                                         in1=r_bc[:], op0=ALU.mult, op1=ALU.mult).then_inc(ht_ready, 1)
                if k >= 1:
                    part(k - 1, gain_next, count)
                if k == 9 and count == 1:
                    split(T_GATE, T_GATE % 2)
                dve.wait_ge(ht_ready, KT * count + k + 1)
                dve.tensor_tensor(h_res[:, k, :], h_res[:, k, :], t_acc[:, k, :], ALU.add).then_inc(h_ready, 1)
            part(KT - 1, gain_next, count)

        def part(k, gain, count):
            g = 1.0 if gain is None else gains[:, gain, k:k + 1]
            gained_rest(k, b_hi, b_lo, h_res, g, b_hi_ready, b_lo_ready, KT * count)

        invert(1)
        dve.wait_ge(h_landed, 64)
        residual(1, 1, 2, 0)
        invert(2)

        for j in range(FF_BLOCKS):
            T0 = T_FF + 2 * KT * j

            def ff1(T, par):
                split(T + 1, 1 - par)
                tile_done(dve, T)
                i = KT * j + T - T0
                dve.scalar_tensor_tensor(out=merged[:, par, :], in0=MM[par][:, 0:TOK], scalar=0.0, in1=r_bc[:],
                                         op0=ALU.max, op1=ALU.mult).then_inc(tiles_drained, 1)
                dve.wait_ge(a_hi_ready, i + (2 * KT + 1))
                dve.tensor_tensor(a_lo[:, T - T0, :], merged[:, par, :], a_hi[:, T - T0, :].bitcast(F32),
                                  ALU.subtract).then_inc(a_lo_ready, 1)

            tiles(dve, T0, T0 + KT - 1, ff1)
            tiles(dve, T0 + KT, T0 + 2 * KT - 1, keep_t(T0 + KT, j > 0))

        split(T_PLE + 1, (T_PLE + 1) % 2)
        dve.wait_ge(p_hi_ready, 1)
        dve.tensor_tensor(p_lo, stage[:], p_hi.bitcast(F32), ALU.subtract).then_inc(p_lo_ready, 1)
        invert(3)
        residual(3, 3, None, 1)

        def gate(T, par, last=False):
            if not last:
                split(T + 1, 1 - par)
            n, j = T - T_GATE, (par - T_GATE) % 2
            dve.wait_ge(tiles_drained, T + 1)
            dve.tensor_tensor(sq[:, par, :], sq[:, par, :], t_acc[:, n, :], ALU.mult).then_inc(gate_pe, 1)
            dve.wait_ge(gate_pe, n + 1)
            dve.wait_ge(y_stored[j], 8 * n + (16 - 8 * j))
            dve.tensor_tensor(merged[:, j, :], sq[:, par, :], h_res[:, n, :], ALU.add).then_inc(y_ready, 1)

        dve.sem_inc(y_stored[0], 16)
        dve.sem_inc(y_stored[1], 16)
        tiles(dve, T_GATE, T_END - 3, gate)
        gate(T_END - 2, (T_END - 2) % 2)
        gate(T_END - 1, (T_END - 1) % 2, last=True)

    @block.gpsimd
    def _(pool):
        for n in by_engine["pool"]:
            pool.sem_inc(h_sem[n], 1)
        pool.memset(ones[:], 1.0)
        pool.memset(eps_col[:], EPS).then_inc(consts_set, 1)
        pool.memset(k_pad[:], 0.0).then_inc(consts_set, 1)

        def square(n, k, src):
            first = isinstance(k, int) and k == 0
            out = sq[:, 1, :] if first else sq[:, 0, :]
            done = pool.tensor_tensor(out, src, src, ALU.mult)
            if first:
                done.then_inc(summed, 1)
                return
            done.then_inc(squared, 1)
            pool.wait_ge(squared, k + (KT - 1) * n)
            pool.wait_ge(summed, k + KT * n)
            pool.tensor_tensor(sq[:, 1, :], sq[:, 1, :], sq[:, 0, :], ALU.add).then_inc(summed, 1)
            pool.wait_ge(summed, k + KT * n + 1)

        def squares(n, wait, src):
            for k in range(KT):
                wait(k)
                if k == 0 and n:
                    pool.wait_ge(norm_sum_ready, n)
                square(n, k, src[:, k, :])

        squares(0, lambda k: pool.wait_ge(x_landed[k // 4], 16), x_in)

        pool.wait_ge(const_landed, 16 * 6)
        pool.wait_ge(tiles_drained, T_V)
        pool.wait_ge(silu_done, 2 + HH)
        pool.wait_ge(hk_ready, 1)
        pool.wait_ge(sample_gates, 1)
        pool.wait_ge(sums_ready, HEADS)

        def head(H, D):
            pool.wait_ge(h_sem["scores_done"], before(H))
            pool.wait_ge(h_sem["so_done"], before(H))
            pool.wait_ge(h_sem["kd_ready"], before(H))
            pool.wait_ge(h_sem["s_new1"], before(H))
            pool.tensor_copy(cum[:], gates[:, H, :])
            pool.tensor_copy(q_b[:], zq[:, H, :])
            pool.tensor_copy(k_b[:], hk[:, H, :] if D == 1 else zk[:, H - HH, :]).then_inc(h_sem["kq_ready"], 1)
            pool.wait_ge(h_sem["s_tok_ready"], now(H))
            pool.wait_ge(h_sem["outer1"], before(H))
            keys = ks_tok[:].rearrange("b (o k) -> b o k", o=1).to_broadcast([NS_TOK, NS_TOK, P])
            on_row = mask8[:].rearrange("b (c o) -> b c o", o=1).to_broadcast([NS_TOK, NS_TOK, P])
            pool.tensor_tensor(k_diag[:], keys, on_row, ALU.mult).then_inc(h_sem["k_diag_ready"], 1)

        with pool.Fori(0, HH) as H:
            head(H, 1)
        with pool.Fori(HH, HEADS) as H:
            head(H, 2)

        squares(1, lambda k: pool.wait_ge(tiles_drained, T_OUT + k + 1), t_acc)
        squares(2, lambda k: pool.wait_ge(h_ready, k + 1), h_res)
        squares(3, lambda k: pool.wait_ge(tiles_drained, T_PLE - KT + k + 1), t_acc)

    ctx.close()


def level_masks():
    s, c = np.arange(P)[:, None], np.arange(64)[None, :]
    return np.concatenate([(s // (2 * h) == c // h) for h in HALF[1:]], axis=1).astype(np.float32)


def kernel(**inputs):
    import concourse.bacc as bacc
    from concourse.bass_utils import run_bass_kernel_spmd

    x = {n: np.ascontiguousarray(a) for n, a in inputs.items()}
    f32 = np.float32

    def by_tile(w):
        k, n = w.shape
        return w.reshape(KT, P, n // P, P).transpose(2, 1, 0, 3).reshape(n // P, P, KT * P)

    w_in = x["w_in"][0]
    edges = np.cumsum([0, HH * P, HH * P, HH * P, HH * P, GH * P, GH * P, GH * GDV, GH * GDV, RANK, D_MODEL, D_MODEL])
    zq, zf, zi, zg, gq, gk, gv, gr, glr, m_h, m_g = [w_in[:, a:b] for a, b in zip(edges[:-1], edges[1:])]
    stream = np.empty((T_END, P, KT * P), f32)
    rank = np.zeros((D_MODEL, P), f32)
    rank[:, 0:RANK] = glr
    stream[T_RANK] = by_tile(rank)[0]
    for at, w in ((T_F, zf), (T_Q, zq), (T_GQ, gq), (T_GK, gk), (T_V, zi), (T_V + HH, gv)):
        stream[at:at + w.shape[1] // P] = by_tile(w)
    m = np.stack([by_tile(m_h), by_tile(m_g)], axis=1).reshape(2 * KT, P, KT * P)
    g, r = by_tile(zg), by_tile(gr)
    for h in range(HH):
        stream[T_HEADS + 4 * h] = g[h]
        stream[T_HEADS + 4 * h + 1:T_HEADS + 4 * h + 4] = m[3 * h:3 * h + 3]
    for h in range(GH):
        at = T_HEADS + 4 * (HH + h)
        stream[at:at + 2] = r[2 * h:2 * h + 2]
        stream[at + 2:at + 4] = m[3 * HH + 2 * h:3 * HH + 2 * h + 2]
    up = np.concatenate([x["w_hgrn_up"][0], x["w_gla_up"][0]], axis=0)
    stream[T_UP:T_OUT] = by_tile(up)
    stream[T_OUT:T_FF] = by_tile(x["w_out"][0])
    for j in range(FF_BLOCKS):
        at, b = T_FF + 2 * KT * j, slice(j * D_MODEL, (j + 1) * D_MODEL)
        stream[at:at + KT] = by_tile(x["w_ff1"][0][:, b])
        stream[at + KT:at + 2 * KT] = by_tile(x["w_ff2"][0][b, :])
    ple = x["w_ple"][0].reshape(2, P, 2, KT // 2, P).transpose(2, 1, 3, 0, 4)
    stream[T_PLE:T_GATE] = ple.reshape(2, P, KT * P)
    stream[T_GATE:T_END] = by_tile(x["w_ple_gate"][0])

    def feature_major(prompt, sample):
        a = np.concatenate([prompt.reshape(NP_TOK, -1), sample.reshape(NS_TOK, -1)], axis=0)
        return np.ascontiguousarray(a.T.reshape(-1, P, TOK).transpose(1, 0, 2))

    norms = [x[n][0].reshape(KT, P).T for n in ("norm_pre_mix", "norm_post_mix", "norm_pre_ffn", "norm_post_ffn")]
    arrays = {
        "x": feature_major(x["x_prompt"], x["x_sample"]),
        "p": feature_major(x["p_prompt"], x["p_sample"]),
        "stream": stream,
        "gains": np.ascontiguousarray(np.stack(norms, axis=1)),
        "head_gain": np.ascontiguousarray(np.concatenate([x["hgrn_norm"].T, x["gla_norm"][0].reshape(2, P).T], axis=1)),
        "gate_w": x["w_gla_gate"][0],
        "gate_b": np.ascontiguousarray(x["b_gla_gate"][0].reshape(GH, P).T),
        "state_hgrn": x["state_hgrn"][0],
        "state_gla": x["state_gla"][0],
        "masks": level_masks(),
        "ident": np.concatenate([np.eye(P, dtype=f32), np.ones((P, P), f32), np.eye(P, dtype=f32)], axis=1),
        "mask8": np.eye(NS_TOK, dtype=f32),
    }
    outs = {
        "y": (P, KT, TOK),
        "new_hgrn_prompt": (HH, P, P),
        "new_gla_prompt": (GH, P, GDV),
        "new_hgrn_sample": (NS_TOK, HH, P, P),
        "new_gla_sample": (NS_TOK, GH, P, GDV),
    }
    nc = bacc.Bacc("TRN2", target_bir_lowering=False, num_devices=1)
    t, sent = {}, {}
    for name, a in arrays.items():
        sent[f"in_{name}"] = a
        t[name] = nc.dram_tensor(f"in_{name}", a.shape, F32, kind="ExternalInput").ap()
    for name, shape in outs.items():
        t[name] = nc.dram_tensor(f"out_{name}", shape, F32, kind="ExternalOutput").ap()
    t["v_spill"] = nc.dram_tensor("v_spill", (P, HH + 2 * GH, TOK), F32, kind="Internal").ap()
    t["m_spill"] = nc.dram_tensor("m_spill", (P, 2 * KT, TOK), F32, kind="Internal").ap()
    build(nc, t)
    got = run_bass_kernel_spmd(nc, [sent], core_ids=[0]).results[0]
    y = got["out_y"].transpose(1, 0, 2).reshape(D_MODEL, TOK).T
    return (np.ascontiguousarray(y[0:NP_TOK]).reshape(x["x_prompt"].shape),
            np.ascontiguousarray(y[NP_TOK:]).reshape(x["x_sample"].shape),
            got["out_new_hgrn_prompt"][None, None], got["out_new_gla_prompt"][None, None],
            got["out_new_hgrn_sample"][None], got["out_new_gla_sample"][None])
```

```python
from contextlib import ExitStack

import numpy as np

import concourse.bass as bass
from concourse import mybir

P = 128
D_MODEL = 2048
KT = D_MODEL // P
NP_TOK = 256
NS_TOK = 8
TOK = NP_TOK + NS_TOK
HH, GH = 8, 4
HEADS = HH + GH
GDV = 256
RANK = 16
D_FF = 4 * D_MODEL
PLE = 256
EPS = 1e-6
GATE_NORM = 16.0
LEVELS = 8
HALF = [P >> l for l in range(LEVELS)]
CELLS = (LEVELS - 1) * 64

HT = KT // 2
SLAB = HT * P
RING = 4

S_GROUP = 32
S_ROWS = 2 * S_GROUP + NS_TOK

T_RANK = 0
T_F = 1
T_Q = T_F + HH
T_GQ = T_Q + HH
T_GK = T_GQ + GH
T_V = T_GK + GH
T_HEADS = T_V + HH + 2 * GH
T_UP = T_HEADS + 4 * HEADS
T_OUT = T_UP + KT
T_FF = T_OUT + KT
FF_BLOCKS = D_FF // D_MODEL
T_PLE = T_FF + 2 * KT * FF_BLOCKS
T_GATE = T_PLE + 2
T_END = T_GATE + KT

F32 = mybir.dt.float32
F32R = mybir.dt.float32r
ALU = mybir.AluOpType
ACT = mybir.ActivationFunctionType


def build(nc, t):
    ctx = ExitStack()

    def sb(name, shape, dt=F32):
        return ctx.enter_context(nc.sbuf_tensor(name, shape, dt))

    def sem(name):
        return ctx.enter_context(nc.semaphore(name))

    raw = sb("raw", [P, RING, SLAB])
    whi = sb("whi", [P, RING, SLAB], F32R)
    wlo = sb("wlo", [P, RING, SLAB], F32R)
    a_hi = sb("a_hi", [P, KT, TOK], F32R)
    a_lo = sb("a_lo", [P, KT, TOK], F32R)
    with nc.sbuf_tensor("before_b", [P, 2 * KT, TOK], F32) as before_b:
        log_gate = before_b[:, 0:HEADS, :]
        hk = before_b[:, KT + HH:2 * KT, :]
    b_hi = sb("b_hi", [P, KT, TOK], F32R)
    b_lo = sb("b_lo", [P, KT, TOK], F32R)
    p_hi, p_lo = a_hi[:, 0:2, :], a_lo[:, 0:2, :]
    room = sb("room", [P, 2 * KT, TOK])
    zf, zq, zk = room[:, 0:HEADS, :], room[:, HEADS:2 * HEADS, :], room[:, 2 * HEADS:2 * HEADS + GH, :]
    gates = zf
    x_in = room[:, HEADS:HEADS + KT, :]
    sgz, sgl = room[:, 2 * HEADS + GH:2 * HEADS + GH + 2, :], room[:, 2 * HEADS + GH + 2:2 * KT, :]
    h_res, t_acc = room[:, 0:KT, :], room[:, KT:2 * KT, :]
    r_bc = sb("r_bc", [P, TOK])
    stage = sb("stage", [P, 2, TOK])
    masks = sb("masks", [P, CELLS])
    ident = sb("ident", [P, 3 * P])
    ones = sb("ones", [P, P])
    gains = sb("gains", [P, 4, KT])
    head_gain = sb("head_gain", [P, 3])
    gate_w = sb("gate_w", [RANK, GH * P])
    gate_b = sb("gate_b", [P, GH])
    own_row = sb("own_row", [S_ROWS, NS_TOK])
    eps_col = sb("eps_col", [P, 1])
    warm = sb("warm", [P, 1])
    v_st = sb("v_st", [P, 2, TOK])
    rank_z = sb("rank_z", [RANK, TOK])
    cum = sb("cum", [P, TOK])
    k_b = sb("k_b", [P, TOK])
    q_b = sb("q_b", [P, TOK])
    kd = sb("kd", [P, NP_TOK])
    kd_tok = sb("kd_tok", [P, 2, P])
    v_tok = sb("v_tok", [P, 2, GDV])
    s_feat = sb("s_feat", [P, 3, 3 * S_GROUP])
    ks_tok = sb("ks_tok", [S_ROWS, P], F32R)
    vs_tok = sb("vs_tok", [S_ROWS, GDV], F32R)
    k_diag = sb("k_diag", [S_ROWS, NS_TOK, P], F32R)
    lev = sb("lev", [P, LEVELS, 2, P])
    after_heads = lev[:].rearrange("c l s t -> c (l s t)")
    m_in = after_heads[:, 0:4 * TOK].rearrange("c (a b t) -> c a b t", a=2, b=2)
    merged = after_heads[:, 4 * TOK:6 * TOK].rearrange("c (a t) -> c a t", a=2)
    k_pad = sb("k_pad", [P, LEVELS - 1, NP_TOK])
    probs = sb("probs", [P, 2, CELLS])
    pairs = sb("pairs", [P, 3, P])
    S = sb("S", [P, 2, 4, GDV])
    s_out = sb("s_out", [P, GDV])
    sq = sb("sq", [P, 2, TOK])
    rs = sb("rs", [P, TOK])
    o_f = sb("o_f", [P, 2, TOK])
    squares = o_f

    bank = [ctx.enter_context(nc.psum_tensor(f"bank{i}", [P, 512], F32)) for i in range(8)]
    MM = bank[0:2]
    SC = bank[2:4]
    DG, TP = bank[4], bank[5]
    O = bank[6:8]

    slab_landed = [sem(f"slab_landed{i}") for i in range(RING)]
    hi_ready = sem("hi_ready")
    lo_ready = sem("lo_ready")
    slabs_multiplied = sem("slabs_multiplied")
    tiles_drained = sem("tiles_drained")
    x_landed = [sem(f"x_landed{i}") for i in range(4)]
    const_landed = sem("const_landed")
    consts_set = sem("consts_set")
    h_landed = sem("h_landed")
    a_hi_ready, a_lo_ready = sem("a_hi_ready"), sem("a_lo_ready")
    b_hi_ready, b_lo_ready = sem("b_hi_ready"), sem("b_lo_ready")
    squared, act_squared, summed = sem("squared"), sem("act_squared"), sem("summed")
    norm_sum_ready, root_ready, r_ready = sem("norm_sum_ready"), sem("root_ready"), sem("r_ready")
    gains_landed = sem("gains_landed")
    gates_ready, gates_stored = sem("gates_ready"), sem("gates_stored")
    silu_done = sem("silu_done")
    ls_abs, ls_exp, ls_ln = sem("ls_abs"), sem("ls_exp"), sem("ls_ln")
    ls_ready, gla_scaled, hk_log, hk_ready = sem("ls_ready"), sem("gla_scaled"), sem("hk_log"), sem("hk_ready")
    sample_gates, sums_ready = sem("sample_gates"), sem("sums_ready")
    stage_stored = [sem("stage_stored0"), sem("stage_stored1")]
    v_landed = sem("v_landed")
    s_landed = [sem("s_landed0"), sem("s_landed1")]
    s_stored = [sem("s_stored0"), sem("s_stored1")]
    state_stored = sem("state_stored")
    by_engine = {
        "act": ["v_tok_ready", "s_tok_ready", "lev_exp", "kd_exp", "kd_tok_ready", "sq_ready",
                "ln_rs", "rs_ready", "o_hi_done", "s_out_ready", "sg_abs", "sg_exp", "sg_ln", "sg_sigma"],
        "dve": ["s_parts_ready", "lev_sub", "lev_ready", "kd_ready", "s_new0", "s_new1", "masked", "probs_ready", "sg_ls",
                "sg_ready", "o_scaled", "o_gated", "o_done"],
        "pe": ["v_turned", "s_turned", "outer0", "outer1", "so_done", "scores_done", "kd_turned",
               "pv_done", "state_done", "ss_done"],
        "pool": ["cum_ready", "kq_ready", "k_diag_ready"],
    }
    h_sem = {n: sem(n) for names in by_engine.values() for n in names}
    m_landed = [sem("m_landed0"), sem("m_landed1")]
    sigma_ready, merge_ready = sem("sigma_ready"), sem("merge_ready")
    ht_ready, h_ready = sem("ht_ready"), sem("h_ready")
    u_ready = sem("u_ready")
    p_landed, p_hi_ready, p_lo_ready = sem("p_landed"), sem("p_hi_ready"), sem("p_lo_ready")
    pe_stored = sem("pe_stored")
    gate_pe, y_ready = sem("gate_pe"), sem("y_ready")
    y_stored = [sem("y_stored0"), sem("y_stored1")]

    def outer_at(D, r, i):
        if D == 1:
            return SC[r][:, i * P:(i + 1) * P]
        return (SC, O)[r][i // 2][:, (i % 2) * GDV:(i % 2 + 1) * GDV]

    PE_BANKS = [SC[0], SC[1], DG, O[0]]
    GATE_BANKS = [DG, O[0], O[1], TP]

    def now(H):
        return H + 2

    def before(H):
        return H + 1

    def tokens(ap, h, side):
        return ap.rearrange("c (p w j) -> c p w j", w=2, j=h)[:, :, side, :]

    def slot_of(par, half):
        return 2 * par + half

    def load_half(sp, T, par, half, first=False):
        s = slot_of(par, half)
        if not first:
            sp.wait_ge(lo_ready, 2 * T + (half - RING + 1))
        sp.dma_start(raw[:, s, :], t["stream"][T, :, half * SLAB:(half + 1) * SLAB]).then_inc(slab_landed[s], 16)

    def load(sp, T, par, first=False):
        for half in range(2):
            load_half(sp, T, par, half, first)

    def round_slab(act, T, par, half, first=False):
        s = slot_of(par, half)
        act.wait_ge(slab_landed[s], 8 * T + (16 - 8 * par))
        if not first:
            act.wait_ge(slabs_multiplied, 2 * T + (half - RING + 1))
        act.copy(whi[:, s, :], raw[:, s, :]).then_inc(hi_ready, 1)

    def rest_slab(dve, T, par, half):
        s = slot_of(par, half)
        dve.wait_ge(hi_ready, 2 * T + (half + 1))
        dve.tensor_tensor(wlo[:, s, :], raw[:, s, :], whi[:, s, :].bitcast(F32), ALU.subtract).then_inc(lo_ready, 1)

    def multiply(pe, T, par, half, out, hi, lo, k0, start, stop, before_k=None, midway=None):
        s = slot_of(par, half)
        pe.wait_ge(lo_ready, 2 * T + (half + 1))
        for k in range(HT):
            if before_k:
                before_k(k0 + k)
            if midway and k == HT // 2:
                midway()
            w = slice(k * P, (k + 1) * P)
            pe.matmul(out, whi[:, s, w], hi[:, k0 + k, :], start=start and k == 0, stop=False)
            pe.matmul(out, whi[:, s, w], lo[:, k0 + k, :], start=False, stop=False)
            mm = pe.matmul(out, wlo[:, s, w], hi[:, k0 + k, :], start=False, stop=stop and k == HT - 1)
        mm.then_inc(slabs_multiplied, 1)

    def tile(pe, T, par, hi, lo, first=False, before_half=None, before_k=None, bank=None):
        if not first:
            pe.wait_ge(tiles_drained, T - 1)
        for half in range(2):
            if before_half:
                before_half(half)
            multiply(pe, T, par, half, (bank or MM)[par][:, 0:TOK], hi, lo, half * HT, half == 0, half == 1, before_k)

    def tile_pair(pe, T, hi, lo, ready, base):
        for k in range(KT):
            half, w = k // HT, slice(k % HT * P, (k % HT + 1) * P)
            pe.wait_ge(ready, base + k + 1)
            for i in range(2):
                if k % HT == 0:
                    pe.wait_ge(lo_ready, 2 * (T + i) + half + 1)
                s, out = slot_of((T + i) % 2, half), MM[(T + i) % 2][:, 0:TOK]
                pe.matmul(out, whi[:, s, w], hi[:, k, :], start=k == 0, stop=False)
                pe.matmul(out, whi[:, s, w], lo[:, k, :], start=False, stop=False)
                mm = pe.matmul(out, wlo[:, s, w], hi[:, k, :], start=False, stop=k == KT - 1)
                if k == HT - 1 and i == 0 or k == KT - 1:
                    mm.then_inc(slabs_multiplied, 2 if k == KT - 1 and i == 0 else 1)

    def tiles(eng, first, last, body):
        with eng.Fori(first, last, 2) as T:
            for j in range(2):
                body(T + j, (first + j) % 2)

    def tile_done(eng, T):
        eng.wait_ge(slabs_multiplied, 2 * T + 2)

    block = ctx.enter_context(nc.Block())

    @block.sync
    def _(sp):
        for i in range(4):
            sp.dma_start(x_in[:, 4 * i:4 * i + 4, :], t["x"][:, 4 * i:4 * i + 4, :]).then_inc(x_landed[i], 16)
            if i == 0:
                sp.dma_start(gains[:], t["gains"]).then_inc(gains_landed, 16)
            if i < 2:
                load(sp, i, i, first=True)
        for dst, name in ((masks, "masks"), (ident, "ident"), (head_gain, "head_gain"), (gate_w, "gate_w"),
                          (gate_b, "gate_b"), (own_row, "own_row")):
            sp.dma_start(dst[:], t[name]).then_inc(const_landed, 16)
        load(sp, 2, 0)
        tiles(sp, 3, T_HEADS + 1, lambda T, par: load(sp, T, par))

        def load_v(H, gla):
            v = t["v_spill"][:, bass.ds(2 * H - HH, 2) if gla else bass.ds(H, 1), :]
            sp.wait_ge(h_sem["v_turned"], before(H))
            sp.dma_start(v_st[:, 0:(2 if gla else 1), :], v).then_inc(v_landed, 16)

        def load_states(H, gla):
            sp.wait_ge(h_sem["so_done"], before(H))
            for r in range(2):
                sp.wait_ge(s_stored[r], 16 * H + 16)
                src = t["state_gla"][4 * r:4 * r + 4, H - HH] if gla else t["state_hgrn"][4 * r:4 * r + 4, H]
                w = GDV if gla else P
                sp.dma_start(S[:, r, :, 0:w], src.rearrange("b k v -> k b v")).then_inc(s_landed[r], 16)

        def head(H, gla, next_gla, more=True):
            T = 4 * H + T_HEADS
            h, w = (H - HH, GDV) if gla else (H, P)
            new = t["new_gla_sample" if gla else "new_hgrn_sample"]

            def m_spill(j):
                at = 2 * H + (HH + j - 2) if gla else 3 * H + (j - 1)
                par = (T_HEADS + j) % 2
                sp.wait_ge(tiles_drained, T + (j + 1))
                sp.dma_start(t["m_spill"][:, at, :], stage[:, par, :]).then_inc(stage_stored[par], 16)

            load(sp, T + 4, (T_HEADS + 4) % 2)
            load_half(sp, T + 5, (T_HEADS + 5) % 2, 0)
            for r in range(2):
                sp.wait_ge(h_sem[f"s_new{r}"], now(H))
                sp.dma_start(new[4 * r:4 * r + 4, h].rearrange("b k v -> k b v"), S[:, r, :, 0:w])\
                  .then_inc(s_stored[r], 16)
            load_half(sp, T + 5, (T_HEADS + 5) % 2, 1)
            if not gla:
                m_spill(1)
            if more:
                load_half(sp, T + 6, (T_HEADS + 6) % 2, 0)
                load_v(H + 1, next_gla)
                load_half(sp, T + 6, (T_HEADS + 6) % 2, 1)
                load_states(H + 1, next_gla)
            m_spill(2)
            if more:
                load(sp, T + 7, (T_HEADS + 7) % 2)
            sp.wait_ge(h_sem["s_out_ready"], now(H))
            sp.dma_start(t["new_gla_prompt" if gla else "new_hgrn_prompt"][h], s_out[:, 0:w])\
              .then_inc(state_stored, 16)
            m_spill(3)

        sp.wait_ge(stage_stored[0], 16 * (1 + HH))
        sp.wait_ge(stage_stored[1], 16 * (1 + HH))
        load_v(0, False)
        load_states(0, False)
        tiles(sp, T_HEADS + 2, T_HEADS + 3, lambda T, par: load(sp, T, par))
        with sp.Fori(0, HH - 1) as H:
            head(H, False, False)
        with sp.Fori(HH - 1, HH) as H:
            head(H, False, True)
        with sp.Fori(HH, HEADS - 1) as H:
            head(H, True, True)
        with sp.Fori(HEADS - 1, HEADS) as H:
            head(H, True, None, more=False)

        sp.wait_ge(stage_stored[0], 16 * (1 + HH + 2 * HH + GH))
        sp.wait_ge(stage_stored[1], 16 * (1 + HH + HH + GH))

        def up_loads(T, par):
            load(sp, T + 2, par)
            sp.wait_ge(merge_ready, T - T_UP + 1)
            sp.dma_start(m_in[:, par_of_m(par), :, :], t["m_spill"][:, bass.ds(2 * (T - T_UP), 2), :])\
              .then_inc(m_landed[par_of_m(par)], 16)

        def par_of_m(par):
            return (par - T_UP) % 2

        tiles(sp, T_UP, T_OUT - 1, up_loads)
        sp.wait_ge(h_sem["o_done"], now(HEADS - 1))
        for i in range(4):
            sp.dma_start(h_res[:, 4 * i:4 * i + 4, :], t["x"][:, 4 * i:4 * i + 4, :]).then_inc(h_landed, 16)
        sp.dma_start(stage[:], t["p"]).then_inc(p_landed, 16)
        tiles(sp, T_OUT + 2, T_GATE + 1, lambda T, par: load(sp, T, par))
        load(sp, T_GATE + 2, T_GATE % 2)

        def store_y(T, par):
            j = (par - T_GATE) % 2
            sp.wait_ge(y_ready, T - T_GATE + 3)
            sp.dma_start(t["y"][:, T - T_GATE, :], merged[:, j, :]).then_inc(y_stored[j], 16)

        def load_and_store(T, par):
            load(sp, T + 3, 1 - par)
            store_y(T, par)

        tiles(sp, T_GATE, T_END - 5, load_and_store)
        load(sp, T_END - 1, (T_END - 1) % 2)
        for T in range(T_END - 4, T_END):
            store_y(T, T % 2)
        for j in range(2):
            sp.wait_ge(y_stored[j], 16 + 16 * KT // 2)
        for r in range(2):
            sp.wait_ge(s_stored[r], 16 * (HEADS + 1))
        sp.wait_ge(state_stored, 16 * (HEADS + 1))

    @block.tensor
    def _(pe):
        for n in by_engine["pe"]:
            pe.sem_inc(h_sem[n], 1)

        tile_pair(pe, T_RANK, a_hi, a_lo, a_lo_ready, 0)
        pe.wait_ge(consts_set, 1)
        pe.wait_ge(summed, KT)
        pe.matmul(TP[:, 0:TOK], ones[:], sq[:, 1, :], start=True, stop=True).then_inc(norm_sum_ready, 1)
        for T in (T_F + 1, T_F + 2):
            tile(pe, T, T % 2, a_hi, a_lo, first=True, bank=SC)
        pe.wait_ge(tiles_drained, 1)
        pe.wait_ge(const_landed, 16 * 6)
        for h in range(GH):
            mm = pe.matmul(GATE_BANKS[h][:, 0:TOK], gate_w[:, h * P:(h + 1) * P], rank_z[:], start=True, stop=True)
        mm.then_inc(gates_ready, 1)
        tile(pe, T_F + 3, (T_F + 3) % 2, a_hi, a_lo)
        tiles(pe, T_F + 4, T_HEADS - 1, lambda T, par: tile(pe, T, par, a_hi, a_lo))

        def turn_v(H, D):
            pe.wait_ge(v_landed, 16 * H + 16)
            pe.wait_ge(h_sem["s_out_ready"], before(H))
            for B in range(2):
                for d in range(D):
                    mm = pe.transpose(TP[:, (B * D + d) * P:(B * D + d + 1) * P], v_st[:, d, B * P:(B + 1) * P],
                                      ident[:, 0:P])
            mm.then_inc(h_sem["v_turned"], 1)

        def turn_s(H, D):
            pe.wait_ge(h_sem["kq_ready"], now(H))
            pe.wait_ge(h_sem["probs_ready"], before(H))
            for i in range(1 + D):
                mm = pe.transpose(SC[1][0:S_ROWS, i * P:(i + 1) * P], s_feat[:, i, 0:S_ROWS], ident[:, 0:P])
            mm.then_inc(h_sem["s_turned"], 1)

        def outer(H, D, r):
            if r == 0:
                pe.wait_ge(h_sem["k_diag_ready"], now(H))
            elif D == 2:
                pe.wait_ge(h_sem["o_scaled"], before(H))
            for i in range(4):
                mm = pe.matmul(outer_at(D, r, i), k_diag[:, 4 * r + i, :], vs_tok[:, 0:D * P], start=True, stop=True)
            mm.then_inc(h_sem[f"outer{r}"], 1)

        def sample_out(H, D, r):
            pe.wait_ge(h_sem["o_scaled"], before(H))
            pe.wait_ge(h_sem["s_new1" if D == 2 else f"s_new{r}"], now(H))
            for i in range(4):
                for d in range(D):
                    b = NP_TOK + 4 * r + i
                    mm = pe.matmul(O[d][:, b:b + 1], S[:, r, i, d * P:(d + 1) * P], q_b[:, b:b + 1],
                                   start=(r == 0 and i == 0), stop=True, skip_group_check=True)
            if r == 1:
                mm.then_inc(h_sem["so_done"], 1)

        def scores(H, D):
            pe.wait_ge(h_sem["lev_ready"], now(H))
            pe.wait_ge(h_sem["s_new1"], now(H))
            pe.wait_ge(h_sem["ln_rs"], before(H))
            for B in range(2):
                at = slice(B * P, (B + 1) * P)
                pe.matmul(DG[:, 2 * B * P:(2 * B + 1) * P], k_b[:, at], q_b[:, at], start=True, stop=True)
                for l in range(1, LEVELS):
                    pe.matmul(SC[B][:, (l - 1) * 64:l * 64], k_pad[:, l - 1, at], lev[:, l, 0, B * 64:(B + 1) * 64],
                              start=True, stop=True)
            pe.matmul(DG[:, P:2 * P], lev[:, 0, 1, :], lev[:, 0, 0, :], start=True, stop=True)\
              .then_inc(h_sem["scores_done"], 1)

        def turn_kd(H):
            pe.wait_ge(h_sem["kd_ready"], now(H))
            pe.wait_ge(h_sem["v_tok_ready"], now(H))
            for B in range(2):
                mm = pe.transpose(TP[:, B * P:(B + 1) * P], kd[:, B * P:(B + 1) * P], ident[:, 0:P])
            mm.then_inc(h_sem["kd_turned"], 1)

        def prob_v(H, D):
            pe.wait_ge(h_sem["probs_ready"], now(H))
            for d in range(D):
                v = slice(d * P, (d + 1) * P)
                pe.matmul(O[d][:, 0:2 * P], v_tok[:, 0, v], pairs[:, 0:2, :], start=False, stop=False, skip_group_check=True)
                mm = pe.matmul(O[d][:, P:2 * P], v_tok[:, 1, v], pairs[:, 2, :], start=False, stop=True, skip_group_check=True)
            mm.then_inc(h_sem["pv_done"], 1)

        def state(H, D):
            pe.wait_ge(h_sem["kd_tok_ready"], now(H))
            for B in range(2):
                mm = pe.matmul(TP[:, 0:D * P], kd_tok[:, B, :], v_tok[:, B, 0:D * P], start=B == 0, stop=B == 1)
            mm.then_inc(h_sem["state_done"], 1)

        def head_norm(H, D):
            pe.wait_ge(h_sem["sq_ready"], now(H))
            for d in range(D):
                mm = pe.matmul(DG[:, 0:TOK], ones[:], sq[:, d, :], start=d == 0, stop=d == D - 1)
            mm.then_inc(h_sem["ss_done"], 1)

        def head(H, D):
            T = 4 * H + T_HEADS

            def slab(k, midway=None):
                j, half = k // 2, k % 2
                par = (T_HEADS + j) % 2
                if half == 0:
                    pe.wait_ge(tiles_drained, T + (j - 1))
                multiply(pe, T + j, par, half, MM[par][:, 0:TOK], a_hi, a_lo, half * HT, half == 0, half == 1, midway=midway)

            slab(0)
            turn_s(H, D)
            turn_v(H, D)
            slab(1)
            slab(2)
            slab(3)
            outer(H, D, 0)
            outer(H, D, 1)
            slab(4)
            slab(5, midway=lambda: scores(H, D))
            turn_kd(H)
            sample_out(H, D, 0)
            slab(6, midway=lambda: sample_out(H, D, 1))
            prob_v(H, D)

            def norm_and_state():
                head_norm(H, D)
                state(H, D)

            slab(7, midway=norm_and_state)

        with pe.Fori(0, HH) as H:
            head(H, 1)
        with pe.Fori(HH, HEADS) as H:
            head(H, 2)

        pe.wait_ge(h_sem["o_done"], now(HH - 1))

        def up(T, par):
            pe.wait_ge(tiles_drained, T - 1)
            multiply(pe, T, par, 0, MM[par][:, 0:TOK], b_hi, b_lo, 0, True, True)
            pe.wait_ge(h_sem["o_done"], now(HEADS - 1))
            multiply(pe, T, par, 1, SC[par][:, 0:TOK], b_hi, b_lo, HT, True, True)

        tiles(pe, T_UP, T_OUT - 1, up)

        def out_proj(T, par):
            tile(pe, T, par, a_hi, a_lo, before_half=lambda half: pe.wait_ge(a_lo_ready, KT + HT * (half + 1)))

        tiles(pe, T_OUT, T_FF - 1, out_proj)

        def norm_sum(n):
            pe.wait_ge(summed, KT * (n + 1))
            pe.matmul(TP[:, 0:TOK], ones[:], sq[:, 1, :], start=True, stop=True).then_inc(norm_sum_ready, 1)

        norm_sum(1)
        for j in range(FF_BLOCKS):
            T0 = T_FF + 2 * KT * j
            if j == 0:
                pe.wait_ge(tiles_drained, T0)
                tile_pair(pe, T0, b_hi, b_lo, b_lo_ready, 0)
                norm_sum(2)
                for T in (T0 + 2, T0 + 3):
                    tile(pe, T, T % 2, b_hi, b_lo, first=True, bank=SC)
            tiles(pe, T0 + 4 * (j == 0), T0 + KT - 1, lambda T, par: tile(pe, T, par, b_hi, b_lo))
            tiles(pe, T0 + KT, T0 + 2 * KT - 1, lambda T, par: tile(
                pe, T, par, a_hi, a_lo,
                before_half=lambda half: pe.wait_ge(a_lo_ready, KT * (2 + j) + HT * (half + 1))))

        norm_sum(3)
        pe.wait_ge(p_lo_ready, 1)
        for i in range(4):
            T, half = T_PLE + i // 2, i % 2
            s = slot_of(T % 2, half)
            pe.wait_ge(lo_ready, 2 * T + half + 1)
            for o in range(4):
                if i >= 1:
                    pe.wait_ge(pe_stored, 4 * (i - 1) + o + 1)
                out = PE_BANKS[o][:, 0:TOK]
                for k in range(2):
                    w = slice((2 * o + k) * P, (2 * o + k + 1) * P)
                    pe.matmul(out, whi[:, s, w], p_hi[:, k, :], start=k == 0, stop=False)
                    pe.matmul(out, whi[:, s, w], p_lo[:, k, :], start=False, stop=False)
                    mm = pe.matmul(out, wlo[:, s, w], p_hi[:, k, :], start=False, stop=k == 1)
            mm.then_inc(slabs_multiplied, 1)
        pe.wait_ge(tiles_drained, T_PLE)
        for j in range(2):
            T = T_GATE + j
            tile(pe, T, T % 2, b_hi, b_lo, first=True, before_k=(lambda k: pe.wait_ge(b_lo_ready, KT + k + 1)) if j == 0 else None)
        tiles(pe, T_GATE + 2, T_END - 1, lambda T, par: tile(pe, T, par, b_hi, b_lo))

    @block.scalar
    def _(act):
        for n in by_engine["act"]:
            act.sem_inc(h_sem[n], 1)
        for s in (*stage_stored, *s_stored, state_stored):
            act.sem_inc(s, 16)

        def split(T, par):
            for half in range(2):
                round_slab(act, T, par, half)

        def square(n, k, src):
            if k == 0:
                if n:
                    act.wait_ge(norm_sum_ready, n)
                act.activation(sq[:, 1, :], src, ACT.Square).then_inc(summed, 1)
                return
            if k > 2:
                act.wait_ge(summed, KT * n + k - 1)
            act.activation(squares[:, k % 2, :], src, ACT.Square).then_inc(act_squared, 1)

        act.wait_ge(gains_landed, 16)
        for k in range(KT):
            if k % 4 == 0:
                act.wait_ge(x_landed[k // 4], 16)
            if k in (2, 4, 6, 8):
                round_slab(act, (k - 2) // 4, (k - 2) // 4, k // 2 % 2 ^ 1, first=True)
            act.activation(a_hi[:, k, :], x_in[:, k, :], ACT.Identity, scale=gains[:, 0, k:k + 1]).then_inc(a_hi_ready, 1)
            square(0, k, x_in[:, k, :])

        def root(n):
            act.activation(warm[:], eps_col[:], ACT.Sqrt)
            act.wait_ge(norm_sum_ready, n + 1)
            act.activation(rs[:], TP[:, 0:TOK], ACT.Sqrt, scale=1.0 / D_MODEL, bias=eps_col[:]).then_inc(root_ready, 1)

        split(2, 0)
        split(3, 1)
        act.wait_ge(consts_set, 1)
        root(0)
        split(4, 0)
        act.wait_ge(gates_ready, 1)
        for h in range(GH):
            src = GATE_BANKS[h][:, 0:TOK]
            act.activation(zf[:, HH + h, :], src, ACT.Identity, bias=gate_b[:, h:h + 1]).then_inc(gates_stored, 1)
        split(5, 1)
        tiles(act, T_F + 4, T_Q - 1, lambda T, par: split(T + 1, 1 - par))

        def q_tile(T, par):
            split(T + 1, 1 - par)
            act.wait_ge(tiles_drained, T + 1)
            act.activation(zq[:, T - T_Q, :], stage[:, par, :], ACT.Silu).then_inc(silu_done, 1)

        tiles(act, T_Q, T_GQ - 1, q_tile)

        for T in range(T_GQ, T_V):
            split(T + 1, 1 - T % 2)
            if T == T_GQ:
                act.wait_ge(tiles_drained, T_Q)
                act.wait_ge(gates_stored, GH)
                act.activation(log_gate, zf, ACT.Abs).then_inc(ls_abs, 1)
            elif T == T_GQ + 1:
                act.wait_ge(ls_abs, 1)
                act.activation(log_gate, log_gate, ACT.Exp, scale=-1.0).then_inc(ls_exp, 1)
            elif T == T_GQ + 2:
                act.wait_ge(ls_exp, 1)
                act.activation(log_gate, log_gate, ACT.Ln, bias=ones[:, 0:1]).then_inc(ls_ln, 1)
            elif T == T_GQ + 5:
                act.wait_ge(hk_log, 1)
                act.activation(hk, hk, ACT.Exp).then_inc(hk_ready, 1)
                act.wait_ge(gla_scaled, 1)
                act.activation(gates[:, :, NP_TOK:TOK], log_gate[:, :, NP_TOK:TOK], ACT.Exp).then_inc(sample_gates, 1)

        def spill(T, par, to, at):
            act.wait_ge(tiles_drained, T + 1)
            act.dma_start(t[to][:, at, :], stage[:, par, :]).then_inc(stage_stored[par], 16)

        def v_tile(T, par):
            split(T + 1, 1 - par)
            spill(T, par, "v_spill", T - T_V)

        tiles(act, T_V, T_HEADS - 1, v_tile)

        act.wait_ge(tiles_drained, T_V)
        act.wait_ge(silu_done, 2 + HH)

        def decays(H):
            act.wait_ge(h_sem["lev_sub"], now(H))
            act.activation(lev[:], lev[:], ACT.Exp).then_inc(h_sem["lev_exp"], 1)
            act.wait_ge(h_sem["cum_ready"], now(H))
            act.wait_ge(h_sem["kd_turned"], before(H))
            act.activation(kd[:], cum[:, 0:NP_TOK], ACT.Exp, scale=-1.0, bias=cum[:, NP_TOK - 1:NP_TOK])\
               .then_inc(h_sem["kd_exp"], 1)

        def head(H, D, more=True):
            T = 4 * H + T_HEADS

            def slab(k):
                round_slab(act, T + (1 + k // 2), (T_HEADS + 1 + k // 2) % 2, k % 2)

            def exp_gate():
                act.wait_ge(tiles_drained, T + D)
                act.wait_ge(h_sem["sg_ready"], before(H))
                e = sgl[:, 0:D, :]
                act.activation(e, sgz[:, 0:D, :], ACT.Abs).then_inc(h_sem["sg_abs"], 1)
                act.wait_ge(h_sem["sg_abs"], now(H))
                act.activation(e, e, ACT.Exp, scale=-1.0).then_inc(h_sem["sg_exp"], 1)

            slab(2)
            act.wait_ge(h_sem["s_turned"], now(H))
            act.wait_ge(h_sem["outer1"], before(H))
            act.copy(ks_tok[:], SC[1][0:S_ROWS, 0:P])
            act.copy(vs_tok[:, 0:D * P], SC[1][0:S_ROWS, P:(1 + D) * P]).then_inc(h_sem["s_tok_ready"], 1)
            act.wait_ge(h_sem["v_turned"], now(H))
            act.wait_ge(h_sem["state_done"], before(H))
            act.copy(v_tok[:, :, 0:D * P], TP[:, 0:2 * D * P].rearrange("s (b v) -> s b v", b=2))\
               .then_inc(h_sem["v_tok_ready"], 1)
            slab(3)
            slab(4)
            if D == 1:
                exp_gate()
            slab(5)
            slab(6)
            if D == 2:
                exp_gate()
            slab(7)
            act.wait_ge(h_sem["kd_turned"], now(H))
            act.copy(kd_tok[:], TP[:, 0:2 * P].rearrange("s (b k) -> s b k", b=2)).then_inc(h_sem["kd_tok_ready"], 1)
            act.wait_ge(h_sem["pv_done"], now(H))
            act.wait_ge(h_sem["ss_done"], before(H))
            for d in range(D):
                sqd = act.activation(sq[:, d, :], O[d][:, 0:TOK], ACT.Square)
            sqd.then_inc(h_sem["sq_ready"], 1)
            if more:
                slab(8)
            act.wait_ge(h_sem["sg_exp"], now(H))
            act.activation(sgl[:, 0:D, :], sgl[:, 0:D, :], ACT.Ln, bias=ones[:, 0:1]).then_inc(h_sem["sg_ln"], 1)
            act.wait_ge(h_sem["ss_done"], now(H))
            act.wait_ge(h_sem["probs_ready"], now(H))
            act.wait_ge(h_sem["o_scaled"], before(H))
            act.activation(rs[:], DG[:, 0:TOK], ACT.Ln, scale=1.0 / (D * P), bias=eps_col[:])\
               .then_inc(h_sem["ln_rs"], 1)
            act.wait_ge(h_sem["state_done"], now(H))
            act.wait_ge(state_stored, 16 * H + 16)
            act.copy(s_out[:, 0:D * P], TP[:, 0:D * P]).then_inc(h_sem["s_out_ready"], 1)
            act.wait_ge(h_sem["ln_rs"], now(H))
            act.activation(rs[:], rs[:], ACT.Exp, scale=-0.5).then_inc(h_sem["rs_ready"], 1)
            act.wait_ge(h_sem["sg_ls"], now(H))
            act.activation(sgl[:, 0:D, :], sgl[:, 0:D, :], ACT.Exp).then_inc(h_sem["sg_sigma"], 1)
            if more:
                slab(9)
                decays(H + 1)
            act.wait_ge(h_sem["o_gated"], now(H))
            k = H if D == 1 else 2 * H - HH
            act.copy(b_hi[:, bass.ds(k, D), :], o_f[:, 0:D, :]).then_inc(h_sem["o_hi_done"], 1)

        decays(0)
        split(T_HEADS + 1, (T_HEADS + 1) % 2)
        with act.Fori(0, HH) as H:
            head(H, 1)
        with act.Fori(HH, HEADS - 1) as H:
            head(H, 2)
        with act.Fori(HEADS - 1, HEADS) as H:
            head(H, 2, more=False)

        def merged_hi(n, m):
            act.wait_ge(merge_ready, n + 3)
            act.copy(a_hi[:, n, :], merged[:, m, :]).then_inc(a_hi_ready, 1)

        def merge(T, par, first=False):
            m = (par - T_UP) % 2
            split(T + 1, 1 - par)
            act.wait_ge(m_landed[m], 8 * (T - T_UP) + (16 - 8 * m))
            act.activation(m_in[:, m, :, :], m_in[:, m, :, :], ACT.Sigmoid).then_inc(sigma_ready, 1)
            if not first:
                merged_hi(T - T_UP - 1, 1 - m)

        merge(T_UP, T_UP % 2, first=True)
        merge(T_UP + 1, 1 - T_UP % 2)
        tiles(act, T_UP + 2, T_OUT - 1, merge)
        merged_hi(KT - 1, 1)
        tiles(act, T_OUT, T_FF - 1, lambda T, par: split(T + 1, 1 - par))
        split(T_FF + 1, (T_FF + 1) % 2)

        root(1)
        for k in range(KT):
            if k == 13:
                round_slab(act, T_FF + 2, T_FF % 2, 0)
            act.wait_ge(h_ready, k + 1)
            act.activation(b_hi[:, k, :], h_res[:, k, :], ACT.Identity, scale=gains[:, 2, k:k + 1])\
               .then_inc(b_hi_ready, 1)
            square(2, k, h_res[:, k, :])
        round_slab(act, T_FF + 2, T_FF % 2, 1)
        split(T_FF + 3, (T_FF + 3) % 2)
        root(2)

        for j in range(FF_BLOCKS):
            T0 = T_FF + 2 * KT * j

            def ff1_part(T, par):
                i = KT * j + T - T0
                act.wait_ge(tiles_drained, T + 1)
                act.activation(merged[:, par, :], merged[:, par, :], ACT.Square).then_inc(u_ready, 1)
                act.wait_ge(u_ready, i + 1)
                act.copy(a_hi[:, T - T0, :], merged[:, par, :]).then_inc(a_hi_ready, 1)

            def ff1(T, par):
                split(T + 1, 1 - par)
                ff1_part(T, par)

            if j == 0:
                for T in range(T0, T0 + 3):
                    ff1_part(T, T % 2)
                ff1(T0 + 3, (T0 + 3) % 2)
            tiles(act, T0 + 4 * (j == 0), T0 + KT - 1, ff1)
            tiles(act, T0 + KT, T0 + 2 * KT - 1, lambda T, par: split(T + 1, 1 - par))

        split(T_PLE + 1, (T_PLE + 1) % 2)
        act.wait_ge(p_landed, 16)
        act.wait_ge(slabs_multiplied, 2 * T_PLE)
        act.copy(p_hi, stage[:]).then_inc(p_hi_ready, 1)
        root(3)
        for k in range(KT):
            act.wait_ge(h_ready, KT + k + 1)
            act.copy(b_hi[:, k, :], h_res[:, k, :]).then_inc(b_hi_ready, 1)
            act.wait_ge(slabs_multiplied, 2 * T_PLE + k // 4 + 1)
            act.copy(t_acc[:, k, :], PE_BANKS[k % 4][:, 0:TOK]).then_inc(pe_stored, 1)
            if k == 7:
                split(T_GATE, T_GATE % 2)
        act.sem_inc(tiles_drained, 2)

        def gate(T, par, last=False):
            if not last:
                split(T + 1, 1 - par)
            tile_done(act, T)
            act.wait_ge(y_ready, T - T_GATE + 1)
            act.activation(sq[:, par, :], MM[par][:, 0:TOK], ACT.Sigmoid).then_inc(tiles_drained, 1)

        tiles(act, T_GATE, T_END - 3, gate)
        gate(T_END - 2, (T_END - 2) % 2)
        gate(T_END - 1, (T_END - 1) % 2, last=True)

    @block.vector
    def _(dve):
        for n in by_engine["dve"]:
            dve.sem_inc(h_sem[n], 1)
        dve.sem_inc(merge_ready, 2)
        dve.sem_inc(y_ready, 2)
        dve.sem_inc(silu_done, 2)

        def split(T, par):
            for half in range(2):
                rest_slab(dve, T, par, half)

        def gained_rest(k, hi, lo, src, gain, ready, done, base=0):
            dve.wait_ge(ready, base + k + 1)
            dve.scalar_tensor_tensor(out=lo[:, k, :], in0=src[:, k, :], scalar=gain, in1=hi[:, k, :].bitcast(F32),
                                     op0=ALU.mult, op1=ALU.subtract).then_inc(done, 1)

        for k in range(KT):
            if k in (2, 4, 6, 8):
                rest_slab(dve, (k - 2) // 4, (k - 2) // 4, k // 2 % 2 ^ 1)
            gained_rest(k, a_hi, a_lo, x_in, gains[:, 0, k:k + 1], a_hi_ready, a_lo_ready)
        split(2, 0)
        split(3, 1)

        def invert(n):
            dve.wait_ge(root_ready, n + 1)
            dve.reciprocal(r_bc[:], rs[:]).then_inc(r_ready, 1)
            dve.wait_ge(r_ready, n + 1)

        def drain(T, par, out, scale=None, rows=P, bank=MM):
            tile_done(dve, T)
            src = bank[par][0:rows, 0:TOK]
            if scale is None:
                return dve.tensor_tensor(out, src, r_bc[0:rows, :], ALU.mult)
            return dve.scalar_tensor_tensor(out=out, in0=src, scalar=scale, in1=r_bc[:], op0=ALU.mult, op1=ALU.mult)

        invert(0)
        drain(0, 0, rank_z[:], rows=RANK).then_inc(tiles_drained, 1)
        drain(T_F, 1, zf[:, 0, :]).then_inc(tiles_drained, 1)
        drain(T_F + 1, 0, zf[:, 1, :], bank=SC).then_inc(tiles_drained, 1)
        split(4, 0)
        drain(T_F + 2, 1, zf[:, 2, :], bank=SC).then_inc(tiles_drained, 1)
        split(5, 1)
        drain(T_F + 3, 0, zf[:, 3, :]).then_inc(tiles_drained, 1)

        def stored(base, dst, scale=None):
            def body(T, par):
                split(T + 1, 1 - par)
                drain(T, par, dst[:, T - base, :], scale).then_inc(tiles_drained, 1)
            return body

        tiles(dve, T_F + 4, T_Q - 1, stored(T_F, zf))

        def q_tile(T, par):
            split(T + 1, 1 - par)
            dve.wait_ge(silu_done, T - T_Q + 1)
            drain(T, par, stage[:, par, :]).then_inc(tiles_drained, 1)

        tiles(dve, T_Q, T_GQ - 1, q_tile)

        def sums(first, last):
            for H in range(first, last):
                dve.tensor_tensor_scan(gates[:, H, 0:NP_TOK], ones[:, 0:1].to_broadcast([P, NP_TOK]),
                                       log_gate[:, H, 0:NP_TOK], 0.0, ALU.mult, ALU.add).then_inc(sums_ready, 1)

        for T in range(T_GQ, T_V):
            (stored(T_GQ - HH, zq, P ** -0.5) if T < T_GK else stored(T_GK, zk))(T, T % 2)
            if T == T_GQ + 3:
                dve.wait_ge(ls_ln, 1)
                dve.scalar_tensor_tensor(out=log_gate, in0=zf, scalar=0.0, in1=log_gate, op0=ALU.min,
                                         op1=ALU.subtract).then_inc(ls_ready, 1)
            elif T == T_GQ + 4:
                dve.wait_ge(ls_ready, 1)
                dve.tensor_tensor(hk, log_gate[:, 0:HH, :], zf[:, 0:HH, :], ALU.subtract).then_inc(hk_log, 1)
                gla = log_gate[:, HH:HEADS, :]
                dve.tensor_scalar(gla, gla, 1.0 / GATE_NORM, None, ALU.mult).then_inc(gla_scaled, 1)
            elif T == T_GQ + 5:
                dve.wait_ge(gla_scaled, 1)
                dve.wait_ge(hk_log, 1)
                sums(0, 4)
            elif T == T_GQ + 6:
                sums(4, 8)
            elif T == T_GQ + 7:
                sums(8, HEADS)
        dve.wait_ge(silu_done, 2 + HH)

        def to_stage(T, par, uses):
            dve.wait_ge(stage_stored[par], 16 * uses + 16)
            drain(T, par, stage[:, par, :]).then_inc(tiles_drained, 1)

        with dve.Fori(0, HH) as i:
            for j in range(2):
                T = 2 * i + (T_V + j)
                par = (T_V + j) % 2
                split(T + 1, 1 - par)
                to_stage(T, par, i)

        dve.wait_ge(gates_stored, GH)
        dve.wait_ge(const_landed, 16 * 6)

        def level_decays(l):
            h = HALF[l]
            pairs = P // h
            left, right = tokens(cum[:, 0:NP_TOK], h, 0), tokens(cum[:, 0:NP_TOK], h, 1)
            mid = left[:, :, h - 1:h].to_broadcast([P, pairs, h])
            dve.tensor_tensor(lev[:, l, 0, :].rearrange("c (p j) -> c p j", j=h), right, mid, ALU.subtract)
            return dve.tensor_tensor(lev[:, l, 1, :].rearrange("c (p j) -> c p j", j=h), mid, left, ALU.subtract)

        def level_half(second):
            for l in range(LEVELS // 2 * second, LEVELS // 2 * (1 + second)):
                last = level_decays(l)
            if second:
                last.then_inc(h_sem["lev_sub"], 1)

        dve.wait_ge(h_sem["cum_ready"], now(0))
        level_half(0)
        level_half(1)

        def head(H, D, more=True):
            T = 4 * H + T_HEADS

            def slab(k):
                rest_slab(dve, T + (1 + k // 2), (T_HEADS + 1 + k // 2) % 2, k % 2)

            def m_tile(j):
                par = (T_HEADS + j) % 2
                if D == 1:
                    uses = H + HH if par else 2 * H + (HH + (j == 3))
                else:
                    uses = H + HH if par else H + 2 * HH
                to_stage(T + j, par, uses)

            def gate_tile(d):
                last = drain(T + d, (T_HEADS + d) % 2, sgz[:, d, :])
                last.then_inc(tiles_drained, 1)

            def new_states(r):
                dve.wait_ge(s_landed[r], 16 * H + 16)
                dve.wait_ge(h_sem[f"outer{r}"], now(H))
                for i in range(4):
                    s, b = S[:, r, i, 0:D * P], NP_TOK + 4 * r + i
                    last = dve.scalar_tensor_tensor(out=s, in0=s, scalar=cum[:, b:b + 1], in1=outer_at(D, r, i),
                                                    op0=ALU.mult, op1=ALU.add)
                last.then_inc(h_sem[f"s_new{r}"], 1)

            def level_operands(l):
                h = HALF[l]
                q, k = tokens(q_b[:, 0:NP_TOK], h, 1), tokens(k_b[:, 0:NP_TOK], h, 0)
                lq = lev[:, l, 0, :].rearrange("c (p j) -> c p j", j=h)
                lk = lev[:, l, 1, :].rearrange("c (p j) -> c p j", j=h)
                dve.tensor_tensor(lq, lq, q, ALU.mult)
                return dve.tensor_tensor(lk if l == 0 else tokens(k_pad[:, l - 1, :], h, 0), lk, k, ALU.mult)

            slab(2)
            dve.wait_ge(h_sem["s_tok_ready"], now(H))
            k_rows, v_rows = slice(2 * S_GROUP, S_ROWS), slice(S_GROUP, S_GROUP + NS_TOK)
            dve.tensor_tensor(ks_tok[k_rows, :], SC[1][k_rows, 0:P], ks_tok[k_rows, :].bitcast(F32), ALU.subtract)
            v_parts = vs_tok[v_rows, 0:D * P]
            dve.tensor_tensor(v_parts, SC[1][v_rows, P:(1 + D) * P], v_parts.bitcast(F32), ALU.subtract)\
               .then_inc(h_sem["s_parts_ready"], 1)
            gate_tile(0)
            dve.wait_ge(h_sem["kq_ready"], now(H))
            dve.wait_ge(h_sem["lev_exp"], now(H))
            for l in range(LEVELS // 2):
                level_operands(l)
            slab(3)
            for l in range(LEVELS // 2, LEVELS):
                last = level_operands(l)
            last.then_inc(h_sem["lev_ready"], 1)
            new_states(0)
            new_states(1)
            dve.wait_ge(h_sem["kd_exp"], now(H))
            dve.tensor_tensor(kd[:], kd[:], k_b[:, 0:NP_TOK], ALU.mult).then_inc(h_sem["kd_ready"], 1)
            slab(4)
            slab(5)
            if D == 1:
                m_tile(1)
            else:
                gate_tile(1)
            slab(6)
            dve.wait_ge(h_sem["scores_done"], now(H))
            dve.wait_ge(h_sem["pv_done"], before(H))
            for B in range(2):
                dve.tensor_tensor(probs[:, B, :], SC[B][:, 0:CELLS], masks[:], ALU.mult).then_inc(h_sem["masked"], 1)
            dve.tensor_tensor(pairs[:], DG[:, 0:3 * P].rearrange("s (b t) -> s b t", b=3),
                              ident[:].rearrange("s (b t) -> s b t", b=3), ALU.mult).then_inc(h_sem["masked"], 1)
            for l in range(1, LEVELS):
                h = HALF[l]
                to = pairs[:, 0:3:2, :].rearrange("s b (p w j) -> s b p w j", w=2, j=h)[:, :, :, 1, :]
                cells = probs[:, :, (l - 1) * 64:l * 64].rearrange("s b (p j) -> s b p j", j=h)
                dve.wait_ge(h_sem["masked"], (LEVELS + 1) * H + (l + 3))
                last = dve.tensor_tensor(to, to, cells, ALU.add)
                last.then_inc(h_sem["probs_ready" if l == LEVELS - 1 else "masked"], 1)
            slab(7)
            m_tile(2)
            if more:
                dve.wait_ge(h_sem["cum_ready"], now(H + 1))
                level_half(0)
                slab(8)
            z, e = sgz[:, 0:D, :], sgl[:, 0:D, :]
            dve.wait_ge(h_sem["sg_ln"], now(H))
            dve.scalar_tensor_tensor(out=e, in0=z, scalar=0.0, in1=e, op0=ALU.min, op1=ALU.subtract)\
               .then_inc(h_sem["sg_ls"], 1)
            if more:
                level_half(1)
                slab(9)
            m_tile(3)
            dve.wait_ge(h_sem["sg_sigma"], now(H))
            dve.tensor_tensor(z, z, e, ALU.mult).then_inc(h_sem["sg_ready"], 1)
            dve.wait_ge(h_sem["rs_ready"], now(H))
            dve.wait_ge(h_sem["o_hi_done"], before(H))
            for d in range(D):
                gain = head_gain[:, (0 if D == 1 else 1 + d):(1 if D == 1 else 2 + d)]
                last = dve.scalar_tensor_tensor(out=o_f[:, d, :], in0=O[d][:, 0:TOK], scalar=gain, in1=rs[:],
                                                op0=ALU.mult, op1=ALU.mult)
            last.then_inc(h_sem["o_scaled"], 1)
            dve.wait_ge(h_sem["o_scaled"], now(H))
            dve.wait_ge(h_sem["sg_ready"], now(H))
            dve.tensor_tensor(o_f[:, 0:D, :], o_f[:, 0:D, :], sgz[:, 0:D, :], ALU.mult).then_inc(h_sem["o_gated"], 1)
            dve.wait_ge(h_sem["o_hi_done"], now(H))
            k = H if D == 1 else 2 * H - HH
            dve.tensor_tensor(b_lo[:, bass.ds(k, D), :], o_f[:, 0:D, :], b_hi[:, bass.ds(k, D), :].bitcast(F32),
                              ALU.subtract).then_inc(h_sem["o_done"], 1)

        split(T_HEADS + 1, (T_HEADS + 1) % 2)
        with dve.Fori(0, HH) as H:
            head(H, 1)
        with dve.Fori(HH, HEADS - 1) as H:
            head(H, 2)
        with dve.Fori(HEADS - 1, HEADS) as H:
            head(H, 2, more=False)

        def merged_lo(n, m):
            dve.wait_ge(a_hi_ready, n + (KT + 1))
            dve.tensor_tensor(a_lo[:, n, :], merged[:, m, :], a_hi[:, n, :].bitcast(F32), ALU.subtract)\
               .then_inc(a_lo_ready, 1)

        def merge(T, par, first=False):
            split(T + 1, 1 - par)
            n, m = T - T_UP, (par - T_UP) % 2
            if not first:
                merged_lo(n - 1, 1 - m)
            tile_done(dve, T)
            dve.wait_ge(sigma_ready, n + 1)
            dve.tensor_tensor(m_in[:, m, 0, :], m_in[:, m, 0, :], MM[par][:, 0:TOK], ALU.mult)
            dve.tensor_tensor(m_in[:, m, 1, :], m_in[:, m, 1, :], SC[par][:, 0:TOK], ALU.mult).then_inc(tiles_drained, 1)
            dve.wait_ge(tiles_drained, T + 1)
            dve.tensor_tensor(merged[:, m, :], m_in[:, m, 0, :], m_in[:, m, 1, :], ALU.add).then_inc(merge_ready, 1)

        merge(T_UP, T_UP % 2, first=True)
        merge(T_UP + 1, 1 - T_UP % 2)
        tiles(dve, T_UP + 2, T_OUT - 1, merge)
        merged_lo(KT - 1, 1)

        def keep_t(T0, add):
            def body(T, par):
                split(T + 1, 1 - par)
                tile_done(dve, T)
                out = t_acc[:, T - T0, :]
                if add:
                    ins = dve.tensor_tensor(out, out, MM[par][:, 0:TOK], ALU.add)
                else:
                    ins = dve.tensor_copy(out, MM[par][:, 0:TOK])
                ins.then_inc(tiles_drained, 1)
            return body

        tiles(dve, T_OUT, T_FF - 1, keep_t(T_OUT, False))

        def residual(gain_at, gain_next, count):
            by_r = r_bc[:].rearrange("c (o t) -> c o t", o=1).to_broadcast([P, 4, TOK])
            chunks = {0: 1, 1: 3, 4: 4, 8: 4, 12: 4}
            for k in range(KT):
                if k in chunks:
                    t_k = t_acc[:, k:k + chunks[k], :]
                    dve.tensor_tensor(t_k, t_k, by_r[:, 0:chunks[k], :], ALU.mult).then_inc(ht_ready, 1)
                    dve.wait_ge(ht_ready, len(chunks) * count + list(chunks).index(k) + 1)
                if k == 1:
                    part(0, gain_next, count)
                dve.scalar_tensor_tensor(out=h_res[:, k, :], in0=t_acc[:, k, :], scalar=gains[:, gain_at, k:k + 1],
                                         in1=h_res[:, k, :], op0=ALU.mult, op1=ALU.add).then_inc(h_ready, 1)
                if k >= 3:
                    part(k - 2, gain_next, count)
                if k == 9 and count == 1:
                    split(T_GATE, T_GATE % 2)
                if k == 13 and count == 0:
                    rest_slab(dve, T_FF + 2, T_FF % 2, 0)
            part(KT - 2, gain_next, count)
            part(KT - 1, gain_next, count)

        def part(k, gain, count):
            g = 1.0 if gain is None else gains[:, gain, k:k + 1]
            gained_rest(k, b_hi, b_lo, h_res, g, b_hi_ready, b_lo_ready, KT * count)

        split(T_FF + 1, (T_FF + 1) % 2)
        invert(1)
        dve.wait_ge(h_landed, 64)
        residual(1, 2, 0)
        rest_slab(dve, T_FF + 2, T_FF % 2, 1)
        split(T_FF + 3, (T_FF + 3) % 2)
        invert(2)

        for j in range(FF_BLOCKS):
            T0 = T_FF + 2 * KT * j

            def ff1_part(T, par, bank=MM):
                tile_done(dve, T)
                i = KT * j + T - T0
                dve.scalar_tensor_tensor(out=merged[:, par, :], in0=bank[par][:, 0:TOK], scalar=0.0, in1=r_bc[:],
                                         op0=ALU.max, op1=ALU.mult).then_inc(tiles_drained, 1)
                dve.wait_ge(a_hi_ready, i + (2 * KT + 1))
                dve.tensor_tensor(a_lo[:, T - T0, :], merged[:, par, :], a_hi[:, T - T0, :].bitcast(F32),
                                  ALU.subtract).then_inc(a_lo_ready, 1)

            def ff1(T, par, bank=MM):
                split(T + 1, 1 - par)
                ff1_part(T, par, bank)

            if j == 0:
                for T in range(T0, T0 + 3):
                    ff1_part(T, T % 2, MM if T < T0 + 2 else SC)
                ff1(T0 + 3, (T0 + 3) % 2, SC)
            tiles(dve, T0 + 4 * (j == 0), T0 + KT - 1, ff1)
            tiles(dve, T0 + KT, T0 + 2 * KT - 1, keep_t(T0 + KT, j > 0))

        split(T_PLE + 1, (T_PLE + 1) % 2)
        dve.wait_ge(p_hi_ready, 1)
        dve.tensor_tensor(p_lo, stage[:], p_hi.bitcast(F32), ALU.subtract).then_inc(p_lo_ready, 1)
        invert(3)
        residual(3, None, 1)

        def gate(T, par, last=False):
            if not last:
                split(T + 1, 1 - par)
            n, j = T - T_GATE, (par - T_GATE) % 2
            dve.wait_ge(tiles_drained, T + 1)
            dve.tensor_tensor(sq[:, par, :], sq[:, par, :], t_acc[:, n, :], ALU.mult).then_inc(gate_pe, 1)
            dve.wait_ge(gate_pe, n + 1)
            dve.wait_ge(y_stored[j], 8 * n + (16 - 8 * j))
            dve.tensor_tensor(merged[:, j, :], sq[:, par, :], h_res[:, n, :], ALU.add).then_inc(y_ready, 1)

        dve.sem_inc(y_stored[0], 16)
        dve.sem_inc(y_stored[1], 16)
        tiles(dve, T_GATE, T_END - 3, gate)
        gate(T_END - 2, (T_END - 2) % 2)
        gate(T_END - 1, (T_END - 1) % 2, last=True)

    @block.gpsimd
    def _(pool):
        for n in by_engine["pool"]:
            pool.sem_inc(h_sem[n], 1)
        pool.memset(ones[:], 1.0)
        pool.memset(eps_col[:], EPS).then_inc(consts_set, 1)
        pool.memset(s_feat[:], 0.0)
        pool.memset(k_pad[:], 0.0).then_inc(consts_set, 1)

        def square(n, k, src):
            first = isinstance(k, int) and k == 0
            out = sq[:, 1, :] if first else sq[:, 0, :]
            done = pool.tensor_tensor(out, src, src, ALU.mult)
            if first:
                done.then_inc(summed, 1)
                return
            done.then_inc(squared, 1)
            pool.wait_ge(squared, k + (KT - 1) * (n // 2))
            pool.wait_ge(summed, k + KT * n)
            pool.tensor_tensor(sq[:, 1, :], sq[:, 1, :], sq[:, 0, :], ALU.add).then_inc(summed, 1)
            pool.wait_ge(summed, k + KT * n + 1)

        def square_all(n, wait, src):
            for k in range(KT):
                wait(k)
                if k == 0:
                    pool.wait_ge(norm_sum_ready, n)
                square(n, k, src[:, k, :])

        def add_squares(n):
            for k in range(1, KT):
                pool.wait_ge(act_squared, (KT - 1) * (n // 2) + k)
                pool.wait_ge(summed, KT * n + k)
                pool.tensor_tensor(sq[:, 1, :], sq[:, 1, :], squares[:, k % 2, :], ALU.add).then_inc(summed, 1)

        add_squares(0)

        pool.wait_ge(const_landed, 16 * 6)
        pool.wait_ge(tiles_drained, T_V)
        pool.wait_ge(silu_done, 2 + HH)
        pool.wait_ge(hk_ready, 1)
        pool.wait_ge(sample_gates, 1)
        pool.wait_ge(sums_ready, HEADS)

        def head(H, D):
            pool.wait_ge(h_sem["kd_ready"], before(H))
            pool.wait_ge(h_sem["s_new1"], before(H))
            pool.tensor_copy(cum[:], gates[:, H, :]).then_inc(h_sem["cum_ready"], 1)
            pool.wait_ge(h_sem["scores_done"], before(H))
            pool.wait_ge(h_sem["so_done"], before(H))
            pool.tensor_copy(q_b[:], zq[:, H, :])
            k = hk[:, H, :] if D == 1 else zk[:, H - HH, :]
            pool.tensor_copy(k_b[:], k)
            pool.wait_ge(v_landed, 16 * H + 16)
            pool.wait_ge(h_sem["s_turned"], before(H))
            for i, src in enumerate([k] + [v_st[:, d, :] for d in range(D)]):
                to = s_feat[:, i, :].rearrange("c (g s) -> c g s", g=3)[:, :, 0:NS_TOK]
                column = src[:, NP_TOK:TOK].rearrange("c (o b) -> c o b", o=1).to_broadcast([P, 3, NS_TOK])
                last = pool.tensor_copy(to, column)
            last.then_inc(h_sem["kq_ready"], 1)
            pool.wait_ge(h_sem["s_parts_ready"], now(H))
            pool.wait_ge(h_sem["outer1"], before(H))
            keys = ks_tok[:].bitcast(F32).rearrange("b (o k) -> b o k", o=1).to_broadcast([S_ROWS, NS_TOK, P])
            on_row = own_row[:].rearrange("b (c o) -> b c o", o=1).to_broadcast([S_ROWS, NS_TOK, P])
            pool.tensor_tensor(k_diag[:], keys, on_row, ALU.mult).then_inc(h_sem["k_diag_ready"], 1)

        with pool.Fori(0, HH) as H:
            head(H, 1)
        with pool.Fori(HH, HEADS) as H:
            head(H, 2)

        square_all(1, lambda k: pool.wait_ge(tiles_drained, T_OUT + k + 1), t_acc)
        add_squares(2)
        square_all(3, lambda k: pool.wait_ge(tiles_drained, T_PLE - KT + k + 1), t_acc)

    ctx.close()


def level_masks():
    s, c = np.arange(P)[:, None], np.arange(64)[None, :]
    return np.concatenate([(s // (2 * h) == c // h) for h in HALF[1:]], axis=1).astype(np.float32)


def kernel(**inputs):
    import concourse.bacc as bacc
    from concourse.bass_utils import run_bass_kernel_spmd

    x = {n: np.ascontiguousarray(a) for n, a in inputs.items()}
    f32 = np.float32

    def by_tile(w):
        k, n = w.shape
        return w.reshape(KT, P, n // P, P).transpose(2, 1, 0, 3).reshape(n // P, P, KT * P)

    w_in = x["w_in"][0]
    edges = np.cumsum([0, HH * P, HH * P, HH * P, HH * P, GH * P, GH * P, GH * GDV, GH * GDV, RANK, D_MODEL, D_MODEL])
    zq, zf, zi, zg, gq, gk, gv, gr, glr, m_h, m_g = [w_in[:, a:b] for a, b in zip(edges[:-1], edges[1:])]
    stream = np.empty((T_END, P, KT * P), f32)
    rank = np.zeros((D_MODEL, P), f32)
    rank[:, 0:RANK] = glr
    stream[T_RANK] = by_tile(rank)[0]
    for at, w in ((T_F, zf), (T_Q, zq), (T_GQ, gq), (T_GK, gk), (T_V, zi), (T_V + HH, gv)):
        stream[at:at + w.shape[1] // P] = by_tile(w)
    m = np.stack([by_tile(m_h), by_tile(m_g)], axis=1).reshape(2 * KT, P, KT * P)
    g, r = by_tile(zg), by_tile(gr)
    for h in range(HH):
        stream[T_HEADS + 4 * h] = g[h]
        stream[T_HEADS + 4 * h + 1:T_HEADS + 4 * h + 4] = m[3 * h:3 * h + 3]
    for h in range(GH):
        at = T_HEADS + 4 * (HH + h)
        stream[at:at + 2] = r[2 * h:2 * h + 2]
        stream[at + 2:at + 4] = m[3 * HH + 2 * h:3 * HH + 2 * h + 2]
    up = np.concatenate([x["w_hgrn_up"][0], x["w_gla_up"][0]], axis=0)
    stream[T_UP:T_OUT] = by_tile(up)
    stream[T_OUT:T_FF] = by_tile(x["w_out"][0])
    for j in range(FF_BLOCKS):
        at, b = T_FF + 2 * KT * j, slice(j * D_MODEL, (j + 1) * D_MODEL)
        stream[at:at + KT] = by_tile(x["w_ff1"][0][:, b])
        stream[at + KT:at + 2 * KT] = by_tile(x["w_ff2"][0][b, :])
    ple = x["w_ple"][0].reshape(2, P, 2, KT // 2, P).transpose(2, 1, 3, 0, 4)
    stream[T_PLE:T_GATE] = ple.reshape(2, P, KT * P)
    stream[T_GATE:T_END] = by_tile(x["w_ple_gate"][0])

    def feature_major(prompt, sample):
        a = np.concatenate([prompt.reshape(NP_TOK, -1), sample.reshape(NS_TOK, -1)], axis=0)
        return np.ascontiguousarray(a.T.reshape(-1, P, TOK).transpose(1, 0, 2))

    norms = [x[n][0].reshape(KT, P).T for n in ("norm_pre_mix", "norm_post_mix", "norm_pre_ffn", "norm_post_ffn")]
    arrays = {
        "x": feature_major(x["x_prompt"], x["x_sample"]),
        "p": feature_major(x["p_prompt"], x["p_sample"]),
        "stream": stream,
        "gains": np.ascontiguousarray(np.stack(norms, axis=1)),
        "head_gain": np.ascontiguousarray(np.concatenate([x["hgrn_norm"].T, x["gla_norm"][0].reshape(2, P).T], axis=1)),
        "gate_w": x["w_gla_gate"][0],
        "gate_b": np.ascontiguousarray(x["b_gla_gate"][0].reshape(GH, P).T),
        "state_hgrn": x["state_hgrn"][0],
        "state_gla": x["state_gla"][0],
        "masks": level_masks(),
        "ident": np.concatenate([np.eye(P, dtype=f32), np.ones((P, P), f32), np.eye(P, dtype=f32)], axis=1),
        "own_row": np.eye(S_GROUP, NS_TOK, dtype=f32)[np.arange(S_ROWS) % S_GROUP],
    }
    outs = {
        "y": (P, KT, TOK),
        "new_hgrn_prompt": (HH, P, P),
        "new_gla_prompt": (GH, P, GDV),
        "new_hgrn_sample": (NS_TOK, HH, P, P),
        "new_gla_sample": (NS_TOK, GH, P, GDV),
    }
    nc = bacc.Bacc("TRN2", target_bir_lowering=False, num_devices=1)
    t, sent = {}, {}
    for name, a in arrays.items():
        sent[f"in_{name}"] = a
        t[name] = nc.dram_tensor(f"in_{name}", a.shape, F32, kind="ExternalInput").ap()
    for name, shape in outs.items():
        t[name] = nc.dram_tensor(f"out_{name}", shape, F32, kind="ExternalOutput").ap()
    t["v_spill"] = nc.dram_tensor("v_spill", (P, HH + 2 * GH, TOK), F32, kind="Internal").ap()
    t["m_spill"] = nc.dram_tensor("m_spill", (P, 2 * KT, TOK), F32, kind="Internal").ap()
    build(nc, t)
    got = run_bass_kernel_spmd(nc, [sent], core_ids=[0]).results[0]
    y = got["out_y"].transpose(1, 0, 2).reshape(D_MODEL, TOK).T
    return (np.ascontiguousarray(y[0:NP_TOK]).reshape(x["x_prompt"].shape),
            np.ascontiguousarray(y[NP_TOK:]).reshape(x["x_sample"].shape),
            got["out_new_hgrn_prompt"][None, None], got["out_new_gla_prompt"][None, None],
            got["out_new_hgrn_sample"][None], got["out_new_gla_sample"][None])
```
